# Optimizing a Trainium2 kernel written in Bass

```python
import jax
import jax.numpy as jnp
from jax import lax
import numpy as np

D_MODEL = 1024
BATCH = 1
SEQ = 256
DEPTH = 2
DEC_BATCH = 8
DEC_SEQ = 8
PAST_LEN = 1024
PAGE_SIZE = 128

N_META = 16
N_HEADS = 16
N_KV_HEADS = 2
HEAD_DIM = D_MODEL // N_HEADS
GROUP = N_HEADS // N_KV_HEADS
ATT_W = N_HEADS * HEAD_DIM
KV_W = N_KV_HEADS * HEAD_DIM
WINDOW = 128
BLOCK = 128
ATT_SCALE = HEAD_DIM ** -0.5
REC_W = 5 * D_MODEL // 4
REC_BLOCKS = 16
REC_BW = REC_W // REC_BLOCKS
CONV_W = 4
LRU_C = 8.0
D_FF = 3 * D_MODEL
N_EXPERTS = 8
TOP_K = 2
EXPERT_FF = 3 * D_MODEL // 2
N_DENSE = (DEPTH + 1) // 2
N_MOE = DEPTH // 2
IN_SIZES = (ATT_W, KV_W, KV_W, REC_W, REC_W, D_MODEL, D_MODEL)
IN_W = sum(IN_SIZES)
RMS_EPS = 1e-6

kernel_name = 'hybrid_swa_sink_rglru_moe_step'

def rmsnorm(x, g):
    xf = x.astype(jnp.float32)
    y = xf * lax.rsqrt(jnp.mean(xf * xf, axis=-1, keepdims=True) + RMS_EPS)
    return (y * g.astype(jnp.float32)).astype(x.dtype)

def swiglu(h, w_gate, w_up, w_down):
    return (jax.nn.silu(h @ w_gate) * (h @ w_up)) @ w_down

def moe_ffn(h, w_router, b_router, w_gate, w_up, w_down):
    logits = (h @ w_router).astype(jnp.float32) + b_router.astype(jnp.float32)
    top_v, top_i = lax.top_k(logits, TOP_K)
    top_w = jax.nn.softmax(top_v, axis=-1)
    combine = jnp.sum(jax.nn.one_hot(top_i, N_EXPERTS, dtype=jnp.float32) * top_w[..., None], axis=-2)
    out = jnp.zeros_like(h)
    for e in range(N_EXPERTS):
        out = out + combine[..., e:e + 1].astype(h.dtype) * swiglu(h, w_gate[e], w_up[e], w_down[e])
    return out

def sink_softmax(s, mask, sinks):
    s = jnp.where(mask, s, -jnp.inf)
    sk = sinks[:, :, None, None]
    m = jnp.maximum(jnp.max(s, axis=-1, keepdims=True), sk)
    p = jnp.exp(s - m)
    return p / (jnp.sum(p, axis=-1, keepdims=True) + jnp.exp(sk - m))

def banded_window_attention(q, k, v, sinks):
    b, l = q.shape[0], q.shape[1]
    pad = (-l) % BLOCK
    lp = l + pad
    nb = lp // BLOCK

    def to_blocks(t, *tail):
        return jnp.pad(t, ((0, 0), (pad, 0), (0, 0), (0, 0))).reshape(b, nb, BLOCK, *tail)

    qb = to_blocks(q, N_KV_HEADS, GROUP, HEAD_DIM)
    kb = to_blocks(k, N_KV_HEADS, HEAD_DIM)
    vb = to_blocks(v, N_KV_HEADS, HEAD_DIM)

    def with_prev(t):
        prev = jnp.concatenate([jnp.zeros_like(t[:, :1]), t[:, :-1]], axis=1)
        return jnp.concatenate([prev, t], axis=2)

    kk = with_prev(kb)
    vv = with_prev(vb)
    qpos = jnp.arange(lp).reshape(nb, BLOCK) - pad
    kpos = qpos[:, :1] - BLOCK + jnp.arange(2 * BLOCK)[None, :]
    d = qpos[:, :, None] - kpos[:, None, :]
    mask = (kpos[:, None, :] >= 0) & (d >= 0) & (d <= WINDOW)
    s = jnp.einsum('bnqkgd,bnskd->bnkgqs', qb, kk, preferred_element_type=jnp.float32) * ATT_SCALE
    p = sink_softmax(s, mask[:, None, None], sinks.reshape(N_KV_HEADS, GROUP).astype(jnp.float32))
    o = jnp.einsum('bnkgqs,bnskd->bnqkgd', p.astype(vv.dtype), vv)
    o = o.reshape(b, lp, ATT_W)[:, pad:]
    return o, k[:, -WINDOW:], v[:, -WINDOW:]

def cached_window_attention(q, k, v, cache_k, cache_v, sinks):
    b, s_new = q.shape[0], q.shape[1]
    kk = jnp.concatenate([cache_k.astype(k.dtype), k], axis=1)
    vv = jnp.concatenate([cache_v.astype(v.dtype), v], axis=1)
    qpos = PAST_LEN + jnp.arange(s_new)
    kpos = PAST_LEN - WINDOW + jnp.arange(WINDOW + s_new)
    d = qpos[:, None] - kpos[None, :]
    mask = (d >= 0) & (d <= WINDOW)
    qg = q.reshape(b, s_new, N_KV_HEADS, GROUP, HEAD_DIM)
    s = jnp.einsum('bqkgd,bskd->bkgqs', qg, kk, preferred_element_type=jnp.float32) * ATT_SCALE
    p = sink_softmax(s, mask, sinks.reshape(N_KV_HEADS, GROUP).astype(jnp.float32))
    o = jnp.einsum('bkgqs,bskd->bqkgd', p.astype(vv.dtype), vv).reshape(b, s_new, ATT_W)
    return o, kk[:, -WINDOW:], vv[:, -WINDOW:]

def rglru_branch(xr, conv_prev, h_prev, pos, w_conv, b_conv, w_a, b_a, w_i, b_i, lam):
    b, l = xr.shape[0], xr.shape[1]
    xp = jnp.concatenate([conv_prev.astype(xr.dtype), xr], axis=1)
    xc = b_conv
    for j in range(CONV_W):
        xc = xc + xp[:, j:j + l] * w_conv[j]
    xb = xc.reshape(b, l, REC_BLOCKS, REC_BW)
    gate_a = jnp.einsum('blnc,ncd->blnd', xb, w_a).reshape(b, l, REC_W) + b_a
    gate_x = jnp.einsum('blnc,ncd->blnd', xb, w_i).reshape(b, l, REC_W) + b_i
    r = jax.nn.sigmoid(gate_a.astype(jnp.float32))
    i = jax.nn.sigmoid(gate_x.astype(jnp.float32))
    log_a = -LRU_C * r * jax.nn.softplus(-lam.astype(jnp.float32))
    a = jnp.exp(log_a)
    mult = jnp.where((pos == 0)[None, :, None], 1.0, jnp.sqrt(-jnp.expm1(2.0 * log_a)))
    bt = mult * i * xc.astype(jnp.float32)
    bt = bt.at[:, 0].add(a[:, 0] * h_prev.astype(jnp.float32))

    def combine(left, right):
        a_l, b_l = left
        a_r, b_r = right
        return a_l * a_r, a_r * b_l + b_r

    _, h = lax.associative_scan(combine, (a, bt), axis=1)
    h = h.astype(xr.dtype)
    return h, h[:, -1], xp[:, -(CONV_W - 1):]

def mixer_block(x, pos, attend, conv_prev, h_prev, p, l):
    b, n = x.shape[0], x.shape[1]
    hn = rmsnorm(x, p['ln_mix'][l])
    z = hn @ p['w_in'][l]
    offs = np.cumsum(IN_SIZES)[:-1].tolist()
    q, k, v, xr, yr, ga, gr = jnp.split(z, offs, axis=-1)
    q = q.reshape(b, n, N_HEADS, HEAD_DIM)
    k = k.reshape(b, n, N_KV_HEADS, HEAD_DIM)
    v = v.reshape(b, n, N_KV_HEADS, HEAD_DIM)
    att, k_state, v_state = attend(l, q, k, v, p['attn_sinks'][l])
    rec, h_last, conv_state = rglru_branch(
        xr, conv_prev, h_prev, pos, p['w_conv'][l], p['b_conv'][l], p['w_rg_a'][l], p['b_rg_a'][l],
        p['w_rg_i'][l], p['b_rg_i'][l], p['rg_lambda'][l])
    rec = rec * jax.nn.gelu(yr)
    merged = jax.nn.sigmoid(ga) * (att @ p['w_att_proj'][l]) + jax.nn.sigmoid(gr) * (rec @ p['w_rec_proj'][l])
    return x + merged @ p['w_out'][l], k_state, v_state, conv_state, h_last

def run_trunk(x, pos, attend, conv_prev, h_prev, p):
    ks, vs, cs, hs = [], [], [], []
    for l in range(DEPTH):
        x, k_s, v_s, c_s, h_s = mixer_block(x, pos, attend, conv_prev[l], h_prev[l], p, l)
        hf = rmsnorm(x, p['ln_ffn'][l])
        j = l // 2
        if l % 2 == 0:
            x = x + swiglu(hf, p['w_ffn_gate'][j], p['w_ffn_up'][j], p['w_ffn_down'][j])
        else:
            x = x + moe_ffn(hf, p['w_router'][j], p['b_router'][j], p['w_exp_gate'][j],
                            p['w_exp_up'][j], p['w_exp_down'][j])
        ks.append(k_s)
        vs.append(v_s)
        cs.append(c_s)
        hs.append(h_s)
    return rmsnorm(x, p['ln_final']), jnp.stack(ks), jnp.stack(vs), jnp.stack(cs), jnp.stack(hs)

def setup_inputs(seed: int = 0) -> dict:
    key = jax.random.key(seed)
    ks = jax.random.split(key, 40)
    f32 = jnp.float32

    def nrm(k, shape, scale):
        return jax.random.normal(k, shape, f32) * scale

    a0 = jax.random.uniform(ks[30], (DEPTH, REC_W), f32, minval=0.9, maxval=0.999)
    s0 = a0 ** (1.0 / LRU_C)
    return {
        'x_prompt': nrm(ks[0], (BATCH, SEQ, D_MODEL), 1.0),
        'x_sample': nrm(ks[1], (DEC_BATCH, DEC_SEQ, D_MODEL), 1.0),
        'cache_k': nrm(ks[2], (DEPTH, DEC_BATCH, WINDOW, N_KV_HEADS, HEAD_DIM), 1.0),
        'cache_v': nrm(ks[3], (DEPTH, DEC_BATCH, WINDOW, N_KV_HEADS, HEAD_DIM), 1.0),
        'state_conv': nrm(ks[4], (DEPTH, DEC_BATCH, CONV_W - 1, REC_W), 1.0),
        'state_rglru': nrm(ks[5], (DEPTH, DEC_BATCH, REC_W), 0.5),
        'meta_tokens': nrm(ks[6], (N_META, D_MODEL), 1.0),
        'ln_mix': 1.0 + nrm(ks[7], (DEPTH, D_MODEL), 0.02),
        'w_in': nrm(ks[8], (DEPTH, D_MODEL, IN_W), D_MODEL ** -0.5),
        'attn_sinks': nrm(ks[9], (DEPTH, N_HEADS), 0.5),
        'w_conv': nrm(ks[10], (DEPTH, CONV_W, REC_W), CONV_W ** -0.5),
        'b_conv': nrm(ks[11], (DEPTH, REC_W), 0.01),
        'w_rg_a': nrm(ks[12], (DEPTH, REC_BLOCKS, REC_BW, REC_BW), REC_BW ** -0.5),
        'b_rg_a': nrm(ks[13], (DEPTH, REC_W), 0.01),
        'w_rg_i': nrm(ks[14], (DEPTH, REC_BLOCKS, REC_BW, REC_BW), REC_BW ** -0.5),
        'b_rg_i': nrm(ks[15], (DEPTH, REC_W), 0.01),
        'rg_lambda': jnp.log(s0) - jnp.log1p(-s0),
        'w_att_proj': nrm(ks[16], (DEPTH, ATT_W, D_MODEL), ATT_W ** -0.5),
        'w_rec_proj': nrm(ks[17], (DEPTH, REC_W, D_MODEL), REC_W ** -0.5),
        'w_out': nrm(ks[18], (DEPTH, D_MODEL, D_MODEL), D_MODEL ** -0.5),
        'ln_ffn': 1.0 + nrm(ks[19], (DEPTH, D_MODEL), 0.02),
        'w_ffn_gate': nrm(ks[20], (N_DENSE, D_MODEL, D_FF), D_MODEL ** -0.5),
        'w_ffn_up': nrm(ks[21], (N_DENSE, D_MODEL, D_FF), D_MODEL ** -0.5),
        'w_ffn_down': nrm(ks[22], (N_DENSE, D_FF, D_MODEL), D_FF ** -0.5),
        'w_router': nrm(ks[23], (N_MOE, D_MODEL, N_EXPERTS), D_MODEL ** -0.5),
        'b_router': nrm(ks[24], (N_MOE, N_EXPERTS), 0.01),
        'w_exp_gate': nrm(ks[25], (N_MOE, N_EXPERTS, D_MODEL, EXPERT_FF), D_MODEL ** -0.5),
        'w_exp_up': nrm(ks[26], (N_MOE, N_EXPERTS, D_MODEL, EXPERT_FF), D_MODEL ** -0.5),
        'w_exp_down': nrm(ks[27], (N_MOE, N_EXPERTS, EXPERT_FF, D_MODEL), EXPERT_FF ** -0.5),
        'ln_final': 1.0 + nrm(ks[28], (D_MODEL,), 0.02),
    }

def reference(x_prompt, x_sample, cache_k, cache_v, state_conv, state_rglru, meta_tokens, ln_mix, w_in,
              attn_sinks, w_conv, b_conv, w_rg_a, b_rg_a, w_rg_i, b_rg_i, rg_lambda, w_att_proj, w_rec_proj,
              w_out, ln_ffn, w_ffn_gate, w_ffn_up, w_ffn_down, w_router, b_router, w_exp_gate, w_exp_up,
              w_exp_down, ln_final):
    p = dict(ln_mix=ln_mix, w_in=w_in, attn_sinks=attn_sinks, w_conv=w_conv, b_conv=b_conv, w_rg_a=w_rg_a,
             b_rg_a=b_rg_a, w_rg_i=w_rg_i, b_rg_i=b_rg_i, rg_lambda=rg_lambda, w_att_proj=w_att_proj,
             w_rec_proj=w_rec_proj, w_out=w_out, ln_ffn=ln_ffn, w_ffn_gate=w_ffn_gate, w_ffn_up=w_ffn_up,
             w_ffn_down=w_ffn_down, w_router=w_router, b_router=b_router, w_exp_gate=w_exp_gate,
             w_exp_up=w_exp_up, w_exp_down=w_exp_down, ln_final=ln_final)

    bp = x_prompt.shape[0]
    meta = jnp.broadcast_to(meta_tokens.astype(x_prompt.dtype)[None], (bp, N_META, D_MODEL))
    xp = jnp.concatenate([meta, x_prompt], axis=1)
    pos_p = jnp.arange(xp.shape[1])
    conv0 = jnp.zeros((DEPTH, bp, CONV_W - 1, REC_W), x_prompt.dtype)
    h0 = jnp.zeros((DEPTH, bp, REC_W), x_prompt.dtype)

    def attend_prompt(l, q, k, v, sinks):
        return banded_window_attention(q, k, v, sinks)

    y_p, new_k_prompt, new_v_prompt, new_conv_prompt, new_h_prompt = run_trunk(
        xp, pos_p, attend_prompt, conv0, h0, p)
    y_prompt = y_p[:, N_META:]

    pos_s = PAST_LEN + jnp.arange(x_sample.shape[1])

    def attend_sample(l, q, k, v, sinks):
        return cached_window_attention(q, k, v, cache_k[l], cache_v[l], sinks)

    y_sample, new_k_sample, new_v_sample, new_conv_sample, new_h_sample = run_trunk(
        x_sample, pos_s, attend_sample, state_conv, state_rglru, p)

    return (y_prompt, y_sample, new_k_prompt, new_v_prompt, new_conv_prompt, new_h_prompt,
            new_k_sample, new_v_sample, new_conv_sample, new_h_sample)


_drawn_inputs = setup_inputs


def setup_inputs(seed=0):
    import zlib

    import numpy as np

    out = dict(_drawn_inputs(seed))
    spreads = {}
    factors = {'attn_sinks': 4.426, 'b_rg_a': 6.026, 'b_rg_i': 8.0, 'ln_final': 2.727}
    for name, (base, spread) in spreads.items():
        noise = np.random.default_rng([zlib.crc32(name.encode()), seed]).standard_normal(out[name].shape)
        drawn = base * np.exp(spread * noise) if base else spread * noise
        out[name] = jnp.asarray(drawn.astype(out[name].dtype))
    for name, factor in factors.items():
        out[name] = (out[name] * factor).astype(out[name].dtype)
    return out
```

```python
from contextlib import ExitStack

import numpy as np

import concourse.bass as bass
from concourse import mybir

F32 = mybir.dt.float32
F32R = mybir.dt.float32r
I32 = mybir.dt.int32
ALU = mybir.AluOpType
ACT = mybir.ActivationFunctionType
AX = mybir.AxisListType.X

P = 128
D = 1024
KD = D // P
META, SEQ, SB, SS = 16, 256, 8, 8
TP = META + SEQ
TS = SB * SS
T = TP + TS
WIN = 128
HD = 64
REC = 1280
KR = REC // P
CW = 4
EP = CW - 1 + SS
EXT = CW - 1 + TP + SB * EP
C = EXT - (CW - 1)
FF = 3072
KF = FF // P
EFF = 1536
NE = 8
SLOTS = 128
EPS = 1e-6
BASE_ADDR = 16512
TT = [(0, 128), (128, 128), (256, T - 256)]

CH = 8 * P
N_IN = 46
N_G, N_A, N_R, N_O = 8, 8, 10, 8
N_MIX = N_IN + N_G + N_A + N_R + N_O
N_FFN = 3 * KF
N_EXP = 36
N_MOE = NE * N_EXP
BASE = [0, N_MIX + N_FFN]
RING, SPLIT = 4, 2
MRING, MSPLIT, LEAD = 9, 4, 3

ATT_UNITS = [("A", u) for u in range(4)] + [("B", u) for u in range(8)] + [("C", 0)] + [("D", u) for u in range(4)]
NU = len(ATT_UNITS)
ATT_W = {"A": 128, "B": 256, "C": 144, "D": 136}
ATT_N = {"A": 4, "B": 2, "C": 2, "D": 2}
SINK0 = {"A": 0, "B": 16, "C": 32, "D": 34}

CONST_SIZES = [("ident", 128), ("ones", 128), ("mA", 256), ("mB", 256), ("mC", 144), ("mD", 136),
               ("tri", 128), ("iota", 128), ("rank", 24), ("valid", 24)]
PAR_SIZES = [("ln_mix", 8), ("ln_ffn", 8), ("w_conv", 40), ("b_conv", 10), ("b_a", 10), ("b_i", 10),
             ("lam", 10), ("sinks", 36)]


def offsets(sizes):
    out, at = {}, 0
    for name, n in sizes:
        out[name] = (at, at + n)
        at += n
    return out, at


CONST, N_CONST = offsets(CONST_SIZES)
PAR, N_PAR = offsets(PAR_SIZES)
GATE_IN = [[0, 1], [0, 1, 2], [1, 2, 3], [2, 3, 4], [3, 4]]
STATE_IN = KR * (SB * 3 + SB)
STATE_OUT = KR * (3 + SB * 3 + 1 + SB)


def build_step(nc, w_mix, w_ffn, w_moe, x_in, consts_in, par_in, misc_in, state_in, kc_in, vc_in,
               o_y, o_kp, o_vp, o_ks, o_vs, o_state):
    with ExitStack() as ctx:
        slab = ctx.enter_context(nc.sbuf_tensor("slab", [P, 212800 // 4], F32))
        base = BASE_ADDR
        used = {}

        def at(name, shape, dt, off):
            n = int(np.prod(shape[1:])) * 4
            assert off + n <= 212800, (name, off + n)
            used[name] = (off, off + n)
            return nc.alloc_sbuf_tensor_at(name, shape, dt, offset=base + off)

        x = at("x", [P, KD, T], F32, 0)
        raw = at("raw", [P, RING, CH], F32, 10752)
        whi = [at(f"whi{i}", [P, 8, P], F32R, 27136 + 8192 * i) for i in range(SPLIT)]
        wlo = [at(f"wlo{i}", [P, 8, P], F32R, 31232 + 8192 * i) for i in range(SPLIT)]
        xnh = at("xnh", [P, KD, T], F32R, 43520)
        xnl = at("xnl", [P, KD, T], F32R, 54272)
        atth = at("atth", [P, KD, T], F32R, 43520)
        attl = at("attl", [P, KD, T], F32R, 54272)
        qkx = at("qkx", [P, 20, T], F32, 65024)
        gates = at("gates", [P, 16, T], F32, 92864)
        yr = at("yr", [P, KR, T], F32, 114368)
        R_, E_, XC_, I_ = 127808, 142208, 156736, 171136
        rg = at("rg", [P, KR, C], F32, R_)
        ext = at("ext", [P, KR, EXT], F32, E_)
        xc = at("xc", [P, KR, C], F32, XC_)
        ig = at("ig", [P, KR, C], F32, I_)
        xch = at("xch", [P, KR, C], F32R, 78464)
        xcl = at("xcl", [P, KR, C], F32R, E_)
        vnew = at("vnew", [SS, SB, P], F32, E_)
        sp = [at(f"sp{i}", [P, 512], F32, E_ + 4096 + 2048 * i) for i in range(2)]
        pt = [at(f"pt{i}", [P, 4, P], F32, E_ + 8192 + 2048 * i) for i in range(2)]
        asq = at("asq", [P, KR, C], F32, E_)
        mul = at("mul", [P, KR, C], F32, 78464)
        hs = at("hs", [P, KR, C], F32, XC_)
        rect = at("rect", [P, KR, T], F32, I_)
        rech = at("rech", [P, KR, T], F32R, E_)
        recl = at("recl", [P, KR, T], F32R, 78464)
        mgh = at("mgh", [P, KD, T], F32R, R_)
        mgl = at("mgl", [P, KD, T], F32R, XC_)
        sq = at("sq", [P, KD, T], F32, I_)
        nt = at("nt", [P, KD, T], F32, E_)
        rms = at("rms", [P, T], F32, E_ + 10752)
        rstd = at("rstd", [P, T], F32, E_ + 12096)
        hfh = at("hfh", [P, KF, T], F32R, 65024)
        hfl = at("hfl", [P, KF, T], F32R, 97280)
        sg = [at(f"sg{i}", [P, T], F32, XC_ + 1344 * i) for i in range(2)]
        hh = at("hh", [P, T], F32, XC_ + 2688)
        tokh = at("tokh", [P, 3, D], F32R, 43520)
        tokl = at("tokl", [P, 3, D], F32R, 55808)
        mwhi = [at(f"mwhi{i}", [P, 2, 512], F32R, 68096 + 8192 * i) for i in range(MSPLIT)]
        mwlo = [at(f"mwlo{i}", [P, 2, 512], F32R, 72192 + 8192 * i) for i in range(MSPLIT)]
        mraw = at("mraw", [P, MRING, CH], F32, 100864)
        xeh = at("xeh", [P, KD, SLOTS], F32R, 10752)
        xel = at("xel", [P, KD, SLOTS], F32R, 14848)
        eh = at("eh", [P, 512], F32, 18944)
        esg = at("esg", [P, 512], F32, 20992)
        yeh = at("yeh", [P, D], F32R, 23040)
        yel = at("yel", [P, D], F32R, 27136)
        hth = at("hth", [P, 4, SLOTS], F32R, 31232)
        htl = at("htl", [P, 4, SLOTS], F32R, 33280)
        sel = at("sel", [P, 3, SLOTS], F32R, 35328)
        selt = at("selt", [P, T], F32R, 36864)
        o = 185536
        kc = at("kc", [P, SB, WIN + SS], F32, o); o += 4352
        vc = at("vc", [P, SB, P], F32, o); o += 4096
        vp = at("vp", [P, 3, P], F32, o); o += 1536
        cst = at("cst", [P, N_CONST], F32, o); o += (N_CONST * 4 + 31) // 32 * 32
        par = at("par", [P, 2, N_PAR], F32, o); o += (2 * N_PAR * 4 + 31) // 32 * 32
        misc = at("misc", [P, 8 + 64 + 24], F32, o); o += 384
        stin = at("stin", [P, STATE_IN], F32, o); o += STATE_IN * 4
        stout = at("stout", [P, STATE_OUT], F32, o); o += STATE_OUT * 4

        qt = at("qt", [P, (TP - 256 + TS) * 8], F32, o); o += 2560

        def small(name, n, dt=F32):
            nonlocal o
            t = at(name, [P, n], dt, o)
            o += (n * 4 + 31) // 32 * 32
            return t

        c1 = small("c1", 20); c2 = small("c2", 20); cm = small("cm", 20)
        sp_e = small("sp_e", 20); sp_z = small("sp_z", 20); sp_p = small("sp_p", 20); sp_q = small("sp_q", 20)
        nsink = small("nsink", 72)
        eps = small("eps", 1)
        mx = [small(f"mx{i}", 4) for i in range(2)]
        neg = [small(f"neg{i}", 4) for i in range(2)]
        dsk = [small(f"dsk{i}", 4) for i in range(2)]
        esk = [small(f"esk{i}", 4) for i in range(2)]
        rsum = [small(f"rsum{i}", 4) for i in range(2)]
        rinv = [small(f"rinv{i}", 4) for i in range(2)]
        lg = small("lg", 24); lg2 = small("lg2", 24); eq = small("eq", 24); oh1 = small("oh1", 24)
        oh2 = small("oh2", 24); top1 = small("top1", 3); top2 = small("top2", 3); rk = small("rk", 3)
        dlt = small("dlt", 3); e2 = small("e2", 3); w1 = small("w1", 3); w2 = small("w2", 3)
        msk = small("msk", 24); cwt = small("cwt", 24); pm = small("pm", 24)
        pmx = small("pmx", 3 * 25); cwx = small("cwx", 3 * 25)
        cur = small("cur", 6); cws = small("cws", 1); cnt = small("cnt", 1); c_a = small("c_a", 1)
        nit = small("nit", 1, I32)

        ps = [ctx.enter_context(nc.psum_tensor(f"ps{i}", [P, 512], F32)) for i in range(8)]

        def sem(name):
            return ctx.enter_context(nc.semaphore(name))

        consts_loaded, x_loaded = sem("consts_loaded"), sem("x_loaded")
        raw_loaded = [sem(f"raw_loaded{i}") for i in range(RING)]
        mraw_loaded = [sem(f"mraw_loaded{i}") for i in range(MRING)]
        hi_done, lo_done, pe_chunk = sem("hi_done"), sem("lo_done"), sem("pe_chunk")
        mhi_done, mlo_done, mpe_chunk = sem("mhi_done"), sem("mlo_done"), sem("mpe_chunk")
        sq_done, sumsq_done, rms_done = sem("sq_done"), sem("sumsq_done"), sem("rms_done")
        nt_done, xhi_done, xlo_done = sem("nt_done"), sem("xhi_done"), sem("xlo_done")
        x_added, z_evac = sem("x_added"), sem("z_evac")
        ext_history, ext_ready, conv_saved, xc_split = sem("ext_history"), sem("ext_ready"), sem("conv_saved"), sem("xc_split")
        gate_evac = sem("gate_evac")
        kcache_loaded, vcache_loaded, state_loaded = sem("kcache_loaded"), sem("vcache_loaded"), sem("state_loaded")
        qt_ready = sem("qt_ready")
        k_ready, vt_mm, v_ready = sem("k_ready"), sem("vt_mm"), sem("v_ready")
        s_mm, s_neg, p_exp, p_norm = sem("s_mm"), sem("s_neg"), sem("p_exp"), sem("p_norm")
        pt_mm, pt_copied, pv_mm, o_hi, o_lo = sem("pt_mm"), sem("pt_copied"), sem("pv_mm"), sem("o_hi"), sem("o_lo")
        ap_post, rp_post, mg_split = sem("ap_post"), sem("rp_post"), sem("mg_split")
        lru_pair, m2_done, m_sqrt = sem("lru_pair"), sem("m2_done"), sem("m_sqrt")
        scan_done, h_saved, rec_split = sem("scan_done"), sem("h_saved"), sem("rec_split")
        ffn_silu, ffn_h, ffn_hi, ffn_lo = sem("ffn_silu"), sem("ffn_h"), sem("ffn_hi"), sem("ffn_lo")
        act_step, dve_step = sem("act_step"), sem("dve_step")
        c_ready, sp_exp = sem("c_ready"), sem("sp_exp")
        tok_mm, tok_hi, tok_lo = sem("tok_mm"), sem("tok_hi"), sem("tok_lo")
        router_mm, top_gap, top_exp, mask_ready = sem("router_mm"), sem("top_gap"), sem("top_exp"), sem("mask_ready")
        pos_mm, rounds_ready = sem("pos_mm"), sem("rounds_ready")
        cur_ready = sem("cur_ready")
        sel_built, g_mm, g_evac, st_mm, st_evac = sem("sel_built"), sem("g_mm"), sem("g_evac"), sem("st_mm"), sem("st_evac")
        m_silu, m_h, t_mm, ht_hi, ht_lo = sem("m_silu"), sem("m_h"), sem("t_mm"), sem("ht_hi"), sem("ht_lo")
        ye_hi, ye_lo, sc_mm, m_add = sem("ye_hi"), sem("ye_lo"), sem("sc_mm"), sem("m_add")
        out_done, kv_out_done, state_out_done = sem("out_done"), sem("kv_out_done"), sem("state_out_done")

        def const(name):
            a, b = CONST[name]
            return cst[:, a:b]

        ident, ones = const("ident"), const("ones")

        def p_(l, name):
            a, b = PAR[name]
            return par[:, l, a:b]

        lnf, wrt, brt = misc[:, 0:8], misc[:, 8:72], misc[:, 72:96]

        def seqs(t):
            end = t.shape[2]
            return t[:, :, end - SB * EP:end].rearrange("p k (b e) -> p k b e", e=EP)

        def gain(n):
            return lnf if n == 4 else p_(n // 2, "ln_ffn" if n % 2 else "ln_mix")

        def att_part(u, tile):
            kind, i = ATT_UNITS[u]
            o = ps[u % 2]
            if kind == "A":
                return tile[:, 2 * i:2 * i + 2, 0:P], o[:, 0:256].rearrange("p (k n) -> p k n", k=2)
            if kind == "B":
                return tile[:, i, P:2 * P], o[:, 0:P]
            first = 2 * P if kind == "C" else TP + 16 * i
            return tile[:, :, first:first + 16], o[:, 0:P].rearrange("p (h s) -> p h s", h=KD)

        block = ctx.enter_context(nc.Block())

        @block.sync
        def _(sy):
            sy.dma_start(x[:, :, :], x_in).then_inc(x_loaded, 16)
            sy.dma_start(cst[:, :], consts_in).then_inc(consts_loaded, 16)
            sy.dma_start(par[:, :, :], par_in).then_inc(consts_loaded, 16)
            sy.dma_start(misc[:, :], misc_in).then_inc(consts_loaded, 16)

            def stream(src, c0, n):
                first = 0
                if c0 == 0:
                    for j in range(RING):
                        sy.dma_start(raw[:, j, :], src[j]).then_inc(raw_loaded[j], 16)
                    first = RING
                with sy.Fori(first // 4, n // 4) as i:
                    for j in range(4):
                        sy.wait_ge(lo_done, i * 4 + (c0 + j + 1 - RING))
                        sy.dma_start(raw[:, (c0 + j) % RING, :], src[i * 4 + j]).then_inc(raw_loaded[(c0 + j) % RING], 16)

            stream(w_mix[0], 0, N_MIX)
            stream(w_ffn, N_MIX, N_FFN)
            stream(w_mix[1], BASE[1], N_MIX)
            sy.wait_ge(pe_chunk, BASE[1] + N_MIX)
            for j in range(MRING):
                sy.dma_start(mraw[:, j, :], w_moe[j]).then_inc(mraw_loaded[j], 16)
            sy.wait_ge(rounds_ready, 1)
            n_round = sy.value_load(nit[0:1, 0:1], min_val=8, max_val=24) // NE
            with sy.Fori(0, n_round) as r:
                with sy.Fori(0, N_MOE // MRING) as i:
                    for j in range(MRING):
                        sy.wait_ge(mlo_done, r * N_MOE + i * MRING + (j + 1))
                        sy.dma_start(mraw[:, j, :], w_moe[i * MRING + (MRING + j)]).then_inc(mraw_loaded[j], 16)
            for j in range(MRING):
                sy.wait_ge(mraw_loaded[j], n_round * (16 * N_MOE // MRING) + 16)
            for k in range(KD):
                sy.wait_ge(nt_done, 4 * KD + k + 1)
                sy.dma_start(o_y[:, k, :], nt[:, k, :]).then_inc(out_done, 16)
            sy.wait_ge(out_done, 16 * KD)

        @block.gpsimd
        def _(pool):
            for l in range(2):
                z0 = N_IN * l
                if l == 1:
                    pool.wait_ge(kv_out_done, 16 * 5)
                    pool.wait_ge(pv_mm, NU)
                pool.dma_start(kc[:, :, 0:WIN], kc_in[l]).then_inc(kcache_loaded, 16)
                pool.dma_start(vc[:, :, :], vc_in[l]).then_inc(vcache_loaded, 16)
                pool.dma_start(stin[:, :], state_in[l]).then_inc(state_loaded, 16)
                pool.wait_ge(xlo_done, 16 * l + 8)
                pool.wait_ge(state_loaded, 16 * (l + 1))
                pool.memset(ext[:, :, 0:3], 0.0).then_inc(ext_history, 1)
                pool.tensor_copy(seqs(ext)[:, :, :, 0:3], stin[:, 0:240].rearrange("p (k b j) -> p k b j", k=KR, b=SB))\
                    .then_inc(ext_history, 1)
                pool.wait_ge(z_evac, z0 + 10)
                pool.wait_ge(kcache_loaded, 16 * (l + 1))
                pool.tensor_copy(kc[:, :, WIN:WIN + SS], qkx[:, 8, TP:T].rearrange("p (b s) -> p b s", b=SB))\
                    .then_inc(k_ready, 1)
                if l == 1:
                    pool.wait_ge(state_out_done, 16)
                pool.wait_ge(ext_ready, 2 * (l + 1))
                pool.tensor_copy(stout[:, 0:30].rearrange("p (k j) -> p k j", k=KR), ext[:, :, TP:TP + 3])\
                    .then_inc(conv_saved, 1)
                pool.tensor_copy(stout[:, 30:270].rearrange("p (k b j) -> p k b j", k=KR, b=SB), seqs(ext)[:, :, :, SS:EP])\
                    .then_inc(conv_saved, 1)
                pool.wait_ge(k_ready, l + 1)
                pool.dma_start(o_kp[l], qkx[:, 8, TP - WIN:TP]).then_inc(kv_out_done, 16)
                pool.dma_start(o_vp[l], qkx[:, 9, TP - WIN:TP]).then_inc(kv_out_done, 16)
                pool.dma_start(o_ks[l], kc[:, :, SS:WIN + SS]).then_inc(kv_out_done, 16)
                pool.wait_ge(vcache_loaded, 16 * (l + 1))
                pool.dma_start(o_vs[l, 0:WIN - SS], vc[SS:WIN, :, :]).then_inc(kv_out_done, 16)
                pool.wait_ge(v_ready, 4 * (l + 1))
                pool.dma_start(o_vs[l, WIN - SS:WIN], vnew[:, :, :]).then_inc(kv_out_done, 16)
                pool.wait_ge(scan_done, KR * (l + 1))
                pool.tensor_copy(stout[:, 270:280].rearrange("p (k j) -> p k j", k=KR), hs[:, :, TP - 1:TP])\
                    .then_inc(h_saved, 1)
                pool.tensor_copy(stout[:, 280:360].rearrange("p (k b) -> p k b", k=KR),
                                 seqs(hs)[:, :, :, EP - 1]).then_inc(h_saved, 1)
                pool.wait_ge(h_saved, 2 * (l + 1))
                pool.wait_ge(conv_saved, 2 * (l + 1))
                pool.dma_start(o_state[l], stout[:, :]).then_inc(state_out_done, 16)
            pool.wait_ge(kv_out_done, 16 * 10)
            pool.wait_ge(state_out_done, 16 * 2)

        @block.scalar
        def _(act):
            def copy(out, in_):
                return nc.scalar.activation(out, in_, ACT.Copy)

            def hi(c, i=0, step=0):
                assert step % RING == 0
                if BASE[1] + N_MIX <= c:
                    return
                act.wait_ge(raw_loaded[c % RING], i * (16 * step // RING) + 16 * (c // RING + 1))
                if c >= SPLIT:
                    act.wait_ge(pe_chunk, i * step + (c - SPLIT + 1))
                copy(whi[c % SPLIT][:, :, :], raw[:, c % RING, :].rearrange("p (k n) -> p k n", n=P)).then_inc(hi_done, 1)

            def norm(n, split=True):
                for k in range(KD):
                    if n == 0:
                        act.wait_ge(x_loaded, 16)
                    elif n < 4:
                        act.wait_ge(x_added, KD * (n - 1) + k + 1)
                    nc.scalar.activation(sq[:, k, :], x[:, k, :], ACT.Square).then_inc(sq_done, 1)
                act.wait_ge(sumsq_done, n + 1)
                nc.scalar.activation(rms[:, :], ps[7][:, 0:T], ACT.Sqrt, bias=eps[:, :], scale=1.0 / D).then_inc(rms_done, 1)
                if split:
                    for k in range(KD):
                        act.wait_ge(nt_done, KD * n + k + 1)
                        copy(xnh[:, k, :], nt[:, k, :]).then_inc(xhi_done, 1)

            act.wait_ge(c_ready, 1)
            nc.scalar.activation(sp_e[:, :], sp_e[:, :], ACT.Exp, scale=-1.0).then_inc(sp_exp, 1)
            act.wait_ge(c_ready, 2)

            hi(0)
            hi(1)
            for l in range(2):
                c0, u0 = BASE[l], NU * l
                norm(2 * l)

                def project(m0, n, out, func):
                    with act.Fori(0, n // 4) as i:
                        for j in range(4):
                            c = c0 + m0 + j
                            hi(c + 2, i, 4)
                            act.wait_ge(pe_chunk, i * 4 + (c + 1))
                            nc.scalar.activation(out[:, bass.ds(i * 4 + j, 1), :], ps[c % 2][:, 0:T], func).then_inc(z_evac, 1)

                project(0, 20, qkx, ACT.Copy)
                project(20, 16, gates, ACT.Sigmoid)
                project(36, 8, yr, ACT.Gelu_apprx_tanh)
                for m in (44, 45):
                    hi(c0 + m + 2)
                    act.wait_ge(pe_chunk, c0 + m + 1)
                    nc.scalar.activation(yr[:, m - 36, :], ps[m % 2][:, 0:T], ACT.Gelu_apprx_tanh).then_inc(z_evac, 1)

                for j in range(N_G):
                    c = c0 + N_IN + j
                    hi(c + 2)
                    act.wait_ge(pe_chunk, c + 1)
                    half, gate, part = j // 4, j // 2 % 2, j % 2
                    dst, bias = (ig, "b_i") if gate else (rg, "b_a")
                    for i in ((3, 4) if part else (0, 1, 2)):
                        t = 5 * half + i
                        nc.scalar.activation(dst[:, t, :], ps[2 + i][:, 0:C], ACT.Sigmoid,
                                             bias=p_(l, bias)[:, t:t + 1]).then_inc(gate_evac, 1)

                act.wait_ge(vt_mm, l + 1)
                copy(vp[:, 0:2, :], ps[0][:, 0:256].rearrange("p (t n) -> p t n", t=2)).then_inc(v_ready, 1)
                copy(vp[0:TP - 256, 2, :], ps[0][0:TP - 256, 256:384]).then_inc(v_ready, 1)
                copy(vnew[:, 0:4, :], ps[1][0:SS, :].rearrange("p (b n) -> p b n", b=4)).then_inc(v_ready, 1)
                copy(vnew[:, 4:8, :], ps[7][0:SS, :].rearrange("p (b n) -> p b n", b=4)).then_inc(v_ready, 1)

                def exps(u):
                    kind, _ = ATT_UNITS[u]
                    n, w, q = ATT_N[kind], ATT_W[kind], u % 2
                    act.wait_ge(s_neg, u0 + u + 1)
                    for i in range(n):
                        nc.scalar.activation(sp[q][:, i * w:(i + 1) * w], sp[q][:, i * w:(i + 1) * w], ACT.Exp,
                                             bias=neg[q][:, i:i + 1], accum_out=rsum[q][:, i:i + 1])
                    nc.scalar.activation(esk[q][:, 0:n], dsk[q][:, 0:n], ACT.Exp).then_inc(p_exp, 1)

                def pt_copy(u):
                    act.wait_ge(pt_mm, u0 + u + 1)
                    src = ps[6 + u % 2][:, :].rearrange("p (i n) -> p i n", i=4)
                    kind, _ = ATT_UNITS[u]
                    if kind in "AB":
                        copy(pt[u % 2][:, :, :], src).then_inc(pt_copied, 2)
                    else:
                        few = ATT_W[kind] - P
                        copy(pt[u % 2][:, 0:2, :], src[:, 0:2, :]).then_inc(pt_copied, 1)
                        copy(pt[u % 2][0:few, 2:4, :], src[0:few, 2:4, :]).then_inc(pt_copied, 1)

                def out_hi(u):
                    act.wait_ge(pv_mm, u0 + u + 1)
                    dst, src = att_part(u, atth)
                    copy(dst, src).then_inc(o_hi, 1)

                for s in range(NU + 2):
                    if s < NU:
                        exps(s)
                    if 1 <= s <= NU:
                        pt_copy(s - 1)
                    if s >= 2:
                        out_hi(s - 2)

                act.wait_ge(kv_out_done, 16 * 5 * (l + 1))
                for j in range(N_A):
                    hi(c0 + 54 + j + 2)
                    if j < 5:
                        for t in (2 * j, 2 * j + 1):
                            k = KR * l + t
                            nc.scalar.activation(asq[:, t, :], rg[:, t, :], ACT.Exp, scale=c2[:, k:k + 1])
                            nc.scalar.activation(mul[:, t, :], rg[:, t, :], ACT.Tanh, scale=cm[:, k:k + 1])
                            ins = nc.scalar.activation(rg[:, t, :], rg[:, t, :], ACT.Exp, scale=c1[:, k:k + 1])
                        ins.then_inc(lru_pair, 1)
                    if j == 5:
                        act.wait_ge(m2_done, 5 * (l + 1))
                        nc.scalar.activation(mul[:, :, :], mul[:, :, :], ACT.Sqrt).then_inc(m_sqrt, 1)
                for j in range(N_R + N_O):
                    hi(c0 + 62 + j + 2)
                norm(2 * l + 1, split=(l == 0))

                if l == 0:
                    f0 = N_MIX

                    def gate_silu(m, i=0):
                        q = m % 2
                        act.wait_ge(pe_chunk, i * 4 + (f0 + 2 * m + 1))
                        if m >= 2:
                            act.wait_ge(ffn_h, i * 2 + (m - 1))
                        nc.scalar.activation(sg[q][:, :], ps[2 * q][:, 0:T], ACT.Silu).then_inc(ffn_silu, 1)

                    for j in range(4):
                        hi(f0 + j + 2)
                        if j % 2 == 0:
                            gate_silu(j // 2)
                    with act.Fori(0, KF // 2 - 1) as i:
                        for j in range(4):
                            hi(f0 + 4 + j + 2, i, 4)
                            if j % 2 == 0:
                                gate_silu(2 + j // 2, i)
                    with act.Fori(0, KF // 4) as i:
                        for j in range(4):
                            hi(f0 + 2 * KF + j + 2, i, 4)

            for t in range(3):
                for f in range(2):
                    n = 2 * t + f
                    rows = TT[t][1]
                    act.wait_ge(tok_mm, n + 1)
                    copy(tokh[0:rows, t, 512 * f:512 * f + 512], ps[n][0:rows, :]).then_inc(tok_hi, 1)
            act.wait_ge(top_gap, 1)
            nc.scalar.activation(e2[:, :], dlt[:, :], ACT.Exp).then_inc(top_exp, 1)
            act.wait_ge(rounds_ready, 1)
            n_it = act.value_load(nit[0:1, 0:1], min_val=8, max_val=24)

            def mhi(q, i=0):
                act.wait_ge(mraw_loaded[q % MRING], i * (16 * N_EXP // MRING) + 16 * (q // MRING + 1))
                if q >= MSPLIT or not isinstance(i, int):
                    act.wait_ge(mpe_chunk, i * N_EXP + (q - MSPLIT + 1))
                copy(mwhi[q % MSPLIT][:, :, :], mraw[:, q % MRING, :].rearrange("p (k n) -> p k n", n=512)).then_inc(mhi_done, 1)

            def gather_evac(f, e):
                act.wait_ge(g_mm, e * 4 + (f + 1))
                dst = (xeh, xel)[f // 2][:, 4 * (f % 2):4 * (f % 2) + 4, :]
                copy(dst, ps[5 + f % 2][:, :].rearrange("p (k n) -> p k n", k=4)).then_inc(g_evac, 1)

            def selt_evac(e):
                act.wait_ge(st_mm, e + 1)
                copy(selt[:, :], ps[7][:, 0:T]).then_inc(st_evac, 1)
                copy(cws[:, :], ps[7][:, 340:341]).then_inc(st_evac, 1)

            for f in range(4):
                gather_evac(f, 0)
            selt_evac(0)
            for q in range(LEAD):
                mhi(q)
            with act.Fori(0, n_it) as i:
                for j in range(N_EXP):
                    act.wait_ge(mraw_loaded[(j + LEAD) % MRING], i * (16 * N_EXP // MRING) + 16 * ((j + LEAD) // MRING + 1))
                    act.wait_ge(mpe_chunk, i * N_EXP + j)
                    copy(mwhi[(j + LEAD) % MSPLIT][:, :, :],
                         mraw[:, (j + LEAD) % MRING, :].rearrange("p (k n) -> p k n", n=512)).then_inc(mhi_done, 1)
                    if j in (3, 11, 23):
                        n = (3, 11, 23).index(j)
                        act.wait_ge(mpe_chunk, i * N_EXP + (j + 1))
                        act.wait_ge(m_h, i * 3 + n)
                        nc.scalar.activation(esg[:, :], ps[0][:, :], ACT.Silu).then_inc(m_silu, 1)
                    if j in (12, 24, 31):
                        n = (12, 24, 31).index(j)
                        act.wait_ge(t_mm, i * 3 + (n + 1))
                        copy(hth[:, :, :], ps[4][:, :].rearrange("p (k n) -> p k n", k=4)).then_inc(ht_hi, 1)
                    if j == 31:
                        gather_evac(0, i + 1)
                        gather_evac(1, i + 1)
                act.wait_ge(mpe_chunk, i * N_EXP + N_EXP)
                act.wait_ge(st_evac, i * 2 + 2)
                for h in range(2):
                    nc.scalar.activation(yeh[:, 512 * h:512 * h + 512], ps[2 + h][:, :], ACT.Copy,
                                         scale=cws[:, 0:1]).then_inc(ye_hi, 1)
                gather_evac(2, i + 1)
                gather_evac(3, i + 1)
                act.wait_ge(ye_lo, i * 2 + 2)
                selt_evac(i + 1)
            act.wait_ge(m_add, n_it * KD)
            norm(4, split=False)


        @block.vector
        def _(ve):
            v = nc.vector
            steps = [0]

            def step(ins):
                steps[0] += 1
                ins.then_inc(dve_step, 1)
                ve.wait_ge(dve_step, steps[0])

            def f32(t):
                return t.bitcast(F32)

            def lo(c, i=0, step_=0):
                assert step_ % RING == 0
                if BASE[1] + N_MIX <= c:
                    return
                ve.wait_ge(hi_done, i * step_ + (c + 1))
                v.tensor_tensor(wlo[c % SPLIT][:, :, :], raw[:, c % RING, :].rearrange("p (k n) -> p k n", n=P),
                                f32(whi[c % SPLIT][:, :, :]), ALU.subtract).then_inc(lo_done, 1)

            def norm(n, split=True):
                g = gain(n)
                ve.wait_ge(rms_done, n + 1)
                step(v.reciprocal(rstd[:, :], rms[:, :]))

                def low(k):
                    ve.wait_ge(xhi_done, KD * n + k + 1)
                    v.tensor_tensor(xnl[:, k, :], nt[:, k, :], f32(xnh[:, k, :]), ALU.subtract).then_inc(xlo_done, 1)

                for k in range(KD):
                    v.scalar_tensor_tensor(out=nt[:, k, :], in0=x[:, k, :], scalar=g[:, k:k + 1], in1=rstd[:, :],
                                           op0=ALU.mult, op1=ALU.mult).then_inc(nt_done, 1)
                    if split and k >= 1:
                        low(k - 1)
                if split:
                    low(KD - 1)

            step(v.memset(eps[:, :], EPS))
            ve.wait_ge(consts_loaded, 48)
            a, b = PAR["lam"]
            lam = par[:, :, a:b]
            two = lambda t: t[:, :].rearrange("p (l k) -> p l k", l=2)
            v.scalar_tensor_tensor(out=two(sp_e), in0=lam, scalar=-1.0, in1=lam, op0=ALU.mult, op1=ALU.max).then_inc(c_ready, 1)
            step(v.tensor_scalar(two(sp_q), lam, -1.0, 0.0, ALU.mult, ALU.max))
            a, b = PAR["sinks"]
            step(v.tensor_scalar(nsink[:, :].rearrange("p (l k) -> p l k", l=2), par[:, :, a:b], -1.0, None, ALU.mult))
            ve.wait_ge(sp_exp, 1)
            step(v.tensor_scalar(sp_p[:, :], sp_e[:, :], 2.0, None, ALU.add))
            step(v.reciprocal(sp_z[:, :], sp_p[:, :]))
            step(v.tensor_tensor(sp_z[:, :], sp_z[:, :], sp_e[:, :], ALU.mult))
            step(v.tensor_tensor(sp_e[:, :], sp_z[:, :], sp_z[:, :], ALU.mult))
            step(v.tensor_scalar(sp_p[:, :], sp_e[:, :], 1.0 / 15, None, ALU.mult))
            for d in (13, 11, 9, 7, 5, 3):
                step(v.scalar_tensor_tensor(out=sp_p[:, :], in0=sp_p[:, :], scalar=1.0 / d, in1=sp_e[:, :], op0=ALU.add, op1=ALU.mult))
            step(v.scalar_tensor_tensor(out=sp_p[:, :], in0=sp_p[:, :], scalar=1.0, in1=sp_z[:, :], op0=ALU.add, op1=ALU.mult))
            step(v.scalar_tensor_tensor(out=sp_p[:, :], in0=sp_p[:, :], scalar=2.0, in1=sp_q[:, :], op0=ALU.mult, op1=ALU.add))
            v.tensor_scalar(c1[:, :], sp_p[:, :], -8.0, None, ALU.mult)
            v.tensor_scalar(c2[:, :], sp_p[:, :], -16.0, None, ALU.mult)
            v.tensor_scalar(cm[:, :], sp_p[:, :], 8.0, None, ALU.mult).then_inc(c_ready, 1)

            lo(0)
            lo(1)
            for l in range(2):
                c0, u0 = BASE[l], NU * l
                norm(2 * l)
                with ve.Fori(0, 5) as i:
                    for j in range(4):
                        lo(c0 + j + 2, i, 4)

                def lines():
                    ve.wait_ge(z_evac, N_IN * l + 20)
                    v.tensor_copy(ext[:, :, 3:3 + TP], qkx[:, 10:20, 0:TP]).then_inc(ext_ready, 1)
                    v.tensor_copy(seqs(ext)[:, :, :, 3:EP],
                                  qkx[:, 10:20, TP:T].rearrange("p k (b s) -> p k b s", b=SB)).then_inc(ext_ready, 1)
                    ve.wait_ge(ext_ready, 2 * (l + 1))
                    ve.wait_ge(ext_history, 2 * (l + 1))

                def conv(t):
                    w = p_(l, "w_conv")
                    step(v.tensor_scalar(xc[:, t, :], ext[:, t, 0:C], w[:, t:t + 1], p_(l, "b_conv")[:, t:t + 1], ALU.mult, ALU.add))
                    for j in range(1, CW):
                        step(v.scalar_tensor_tensor(out=xc[:, t, :], in0=ext[:, t, j:j + C], scalar=w[:, KR * j + t:KR * j + t + 1],
                                                    in1=xc[:, t, :], op0=ALU.mult, op1=ALU.add))
                    step(v.tensor_copy(xch[:, t, :], xc[:, t, :]))
                    if t == 0:
                        ve.wait_ge(conv_saved, 2 * (l + 1))
                    v.tensor_tensor(xcl[:, t, :], xc[:, t, :], f32(xch[:, t, :]), ALU.subtract).then_inc(xc_split, 1)

                for j in range(20, N_IN + N_G):
                    lo(c0 + j + 2)
                    if j == 20:
                        lines()
                    if 21 <= j < 41 and j % 2:
                        conv((j - 21) // 2)
                ve.wait_ge(z_evac, N_IN * l + 10)
                v.tensor_copy(qt[:, 0:128].rearrange("p (h s) -> p h s", h=KD), qkx[:, 0:8, 256:TP])
                v.tensor_copy(qt[:, 128:].rearrange("p (b h s) -> p h b s", b=SB, h=KD),
                              qkx[:, 0:8, TP:T].rearrange("p h (b s) -> p h b s", b=SB)).then_inc(qt_ready, 1)
                ve.wait_ge(gate_evac, 20 * (l + 1))
                step(v.tensor_tensor(ig[:, :, :], ig[:, :, :], xc[:, :, :], ALU.mult))

                def maxima(u):
                    kind, k = ATT_UNITS[u]
                    n, w, q = ATT_N[kind], ATT_W[kind], u % 2
                    mask = const("m" + kind)
                    s0 = SINK0[kind] + (n * k if kind in "AB" else 0)
                    ns = nsink[:, 36 * l + s0:36 * l + s0 + n]
                    ve.wait_ge(s_mm, u0 + u + 1)
                    if u >= 2:
                        ve.wait_ge(pt_mm, u0 + u - 1)
                    if kind == "D":
                        for g in range(2):
                            r = slice(64 * g, 64 * g + 64)
                            ins = v.scalar_tensor_tensor(
                                out=sp[q][r, 0:n * w].rearrange("p (i w) -> p i w", i=n),
                                in0=ps[2 + 2 * q + g][r, 0:n * w].rearrange("p (i w) -> p i w", i=n), scalar=HD ** -0.5,
                                in1=mask[r, :].unsqueeze(1).to_broadcast([64, n, w]), op0=ALU.mult, op1=ALU.add)
                    else:
                        per = n * w // 2
                        for g in range(2):
                            ins = v.scalar_tensor_tensor(
                                out=sp[q][:, g * per:(g + 1) * per], in0=ps[2 + 2 * q + g][:, 0:per], scalar=HD ** -0.5,
                                in1=mask[:, 0:per], op0=ALU.mult, op1=ALU.add)
                    step(ins)
                    step(v.tensor_reduce(mx[q][:, 0:n], sp[q][:, 0:n * w].rearrange("p (i w) -> p i w", i=n), AX, ALU.max))
                    step(v.scalar_tensor_tensor(out=neg[q][:, 0:n], in0=mx[q][:, 0:n], scalar=-1.0, in1=ns, op0=ALU.mult, op1=ALU.min))
                    v.tensor_tensor(dsk[q][:, 0:n], neg[q][:, 0:n], ns, ALU.subtract).then_inc(s_neg, 1)

                def weights(u):
                    kind, _ = ATT_UNITS[u]
                    n, w, q = ATT_N[kind], ATT_W[kind], u % 2
                    ve.wait_ge(p_exp, u0 + u + 1)
                    step(v.tensor_tensor(rinv[q][:, 0:n], rsum[q][:, 0:n], esk[q][:, 0:n], ALU.add))
                    step(v.reciprocal(rinv[q][:, 0:n], rinv[q][:, 0:n]))
                    for i in range(n):
                        ins = v.tensor_scalar(sp[q][:, i * w:(i + 1) * w], sp[q][:, i * w:(i + 1) * w], rinv[q][:, i:i + 1], None, ALU.mult)
                    ins.then_inc(p_norm, 1)

                def out_lo(u):
                    ve.wait_ge(o_hi, u0 + u + 1)
                    dst, src = att_part(u, attl)
                    v.tensor_tensor(dst, src, f32(att_part(u, atth)[0]), ALU.subtract).then_inc(o_lo, 1)

                for s in range(NU + 3):
                    if s < NU:
                        maxima(s)
                    if 1 <= s <= NU:
                        weights(s - 1)
                    if s >= 3:
                        out_lo(s - 3)

                for j in range(N_A):
                    c = c0 + 54 + j
                    lo(c + 2)
                    ve.wait_ge(pe_chunk, c + 1)
                    v.tensor_tensor(gates[:, j, :], ps[j % 2][:, 0:T], gates[:, j, :], ALU.mult).then_inc(ap_post, 1)
                    if 1 <= j <= 5:
                        ve.wait_ge(lru_pair, 5 * l + j)
                        pair = slice(2 * (j - 1), 2 * j)
                        v.scalar_tensor_tensor(out=mul[:, pair, :], in0=asq[:, pair, :], scalar=1.0, in1=mul[:, pair, :],
                                               op0=ALU.add, op1=ALU.mult).then_inc(m2_done, 1)
                v.memset(seqs(rg)[:, :, :, 2], 0.0)
                ve.wait_ge(m_sqrt, l + 1)
                step(v.memset(mul[:, :, 0:1], 1.0))
                step(v.tensor_tensor(ig[:, :, :], ig[:, :, :], mul[:, :, :], ALU.mult))
                ve.wait_ge(state_loaded, 16 * (l + 1))
                step(v.tensor_copy(seqs(ig)[:, :, :, 2], stin[:, 240:320].rearrange("p (k b) -> p k b", k=KR)))
                for t in range(KR):
                    v.tensor_tensor_scan(hs[:, t, :], rg[:, t, :], ig[:, t, :], 0.0, ALU.mult, ALU.add).then_inc(scan_done, 1)
                ve.wait_ge(scan_done, KR * (l + 1))
                v.tensor_tensor(rect[:, :, 0:TP], hs[:, :, 0:TP], yr[:, :, 0:TP], ALU.mult)
                step(v.tensor_tensor(rect[:, :, TP:T].rearrange("p k (b s) -> p k b s", b=SB), seqs(hs)[:, :, :, 3:EP],
                                     yr[:, :, TP:T].rearrange("p k (b s) -> p k b s", b=SB), ALU.mult))
                step(v.tensor_copy(rech[:, :, :], rect[:, :, :]))
                v.tensor_tensor(recl[:, :, :], rect[:, :, :], f32(rech[:, :, :]), ALU.subtract).then_inc(rec_split, 1)

                ve.wait_ge(h_saved, 2 * (l + 1))
                m = 0
                for j in range(N_R):
                    c = c0 + 62 + j
                    lo(c + 2)
                    while m < KD and (KR * m + KR - 1) // 8 == j:
                        ve.wait_ge(pe_chunk, c + 1)
                        ins = v.tensor_tensor(gates[:, KD + m, :], ps[m % 2][:, 0:T], gates[:, KD + m, :], ALU.mult)
                        ins.then_inc(rp_post, 1)
                        ve.wait_ge(rp_post, KD * l + m + 1)
                        step(v.tensor_tensor(gates[:, m, :], gates[:, m, :], gates[:, KD + m, :], ALU.add))
                        step(v.tensor_copy(mgh[:, m, :], gates[:, m, :]))
                        v.tensor_tensor(mgl[:, m, :], gates[:, m, :], f32(mgh[:, m, :]), ALU.subtract).then_inc(mg_split, 1)
                        m += 1

                for m in range(KD):
                    c = c0 + 72 + m
                    lo(c + 2)
                    ve.wait_ge(pe_chunk, c + 1)
                    v.tensor_tensor(x[:, m, :], ps[m % 2][:, 0:T], x[:, m, :], ALU.add).then_inc(x_added, 1)
                norm(2 * l + 1, split=(l == 0))

                if l == 0:
                    f0 = N_MIX

                    def hidden(m, i=0):
                        q = m % 2
                        ve.wait_ge(pe_chunk, i * 4 + (f0 + 2 * m + 2))
                        ve.wait_ge(ffn_silu, i * 2 + (m + 1))
                        ve.wait_ge(ffn_lo, i * 2 + m)
                        v.tensor_tensor(hh[:, :], ps[2 * q + 1][:, 0:T], sg[q][:, :], ALU.mult).then_inc(ffn_h, 1)
                        ve.wait_ge(ffn_h, i * 2 + (m + 1))
                        v.tensor_copy(hfh[:, bass.ds(i * 2 + m, 1), :], hh[:, :].unsqueeze(1)).then_inc(ffn_hi, 1)
                        ve.wait_ge(ffn_hi, i * 2 + (m + 1))
                        v.tensor_tensor(hfl[:, bass.ds(i * 2 + m, 1), :], hh[:, :].unsqueeze(1),
                                        f32(hfh[:, bass.ds(i * 2 + m, 1), :]), ALU.subtract).then_inc(ffn_lo, 1)

                    with ve.Fori(0, KF // 2) as i:
                        for j in range(4):
                            lo(f0 + j + 2, i, 4)
                            if j % 2:
                                hidden(j // 2, i)
                    with ve.Fori(0, 2) as i:
                        for j in range(12):
                            c = f0 + 2 * KF + j
                            lo(c + 2, i, 12)
                            if j % 3 == 2:
                                m = j // 3
                                ve.wait_ge(pe_chunk, i * 12 + (c + 1))
                                xm = x[:, bass.ds(i * 4 + m, 1), :]
                                v.tensor_tensor(xm, ps[4 + m % 2][:, 0:T].unsqueeze(1), xm, ALU.add).then_inc(x_added, 1)

            for t in range(3):
                for f in range(2):
                    n = 2 * t + f
                    rows = TT[t][1]
                    ve.wait_ge(tok_hi, n + 1)
                    v.tensor_tensor(tokl[0:rows, t, 512 * f:512 * f + 512], ps[n][0:rows, :],
                                    f32(tokh[0:rows, t, 512 * f:512 * f + 512]), ALU.subtract).then_inc(tok_lo, 1)

            def e3(t):
                return t[:, :].rearrange("p (t e) -> p t e", e=NE)

            def per_row(t):
                return t[:, :].unsqueeze(2).to_broadcast([P, 3, NE])

            step(v.memset(lg[:, :], 0.0))
            ve.wait_ge(router_mm, 1)
            rows = TT[2][1]
            v.tensor_tensor(lg[:, 0:16], ps[6][:, 0:16], brt[:, 0:16], ALU.add)
            step(v.tensor_tensor(lg[0:rows, 16:24], ps[6][0:rows, 16:24], brt[0:rows, 16:24], ALU.add))
            rank = const("rank")

            def largest(lgt, top, oh):
                step(v.tensor_reduce(top[:, :], e3(lgt), AX, ALU.max))
                step(v.tensor_tensor(e3(eq), e3(lgt), per_row(top), ALU.is_equal))
                step(v.tensor_tensor(eq[:, :], eq[:, :], rank, ALU.mult))
                step(v.tensor_reduce(rk[:, :], e3(eq), AX, ALU.max))
                step(v.tensor_tensor(e3(oh), rank.rearrange("p (t e) -> p t e", e=NE), per_row(rk), ALU.is_equal))

            largest(lg, top1, oh1)
            step(v.scalar_tensor_tensor(out=lg2[:, :], in0=oh1[:, :], scalar=-3.0e38, in1=lg[:, :], op0=ALU.mult, op1=ALU.add))
            largest(lg2, top2, oh2)
            v.tensor_tensor(dlt[:, :], top2[:, :], top1[:, :], ALU.subtract).then_inc(top_gap, 1)
            step(v.tensor_tensor(msk[:, :], oh1[:, :], oh2[:, :], ALU.add))
            v.tensor_tensor(msk[:, :], msk[:, :], const("valid"), ALU.mult).then_inc(mask_ready, 1)
            ve.wait_ge(top_exp, 1)
            step(v.tensor_scalar(w1[:, :], e2[:, :], 1.0, None, ALU.add))
            step(v.reciprocal(w1[:, :], w1[:, :]))
            step(v.tensor_tensor(w2[:, :], e2[:, :], w1[:, :], ALU.mult))
            step(v.tensor_tensor(e3(oh1), e3(oh1), per_row(w1), ALU.mult))
            step(v.tensor_tensor(e3(oh2), e3(oh2), per_row(w2), ALU.mult))
            step(v.tensor_tensor(cwt[:, :], oh1[:, :], oh2[:, :], ALU.add))
            ve.wait_ge(pos_mm, 1)
            step(v.scalar_tensor_tensor(out=pm[:, :], in0=ps[7][:, 0:24], scalar=1.0, in1=msk[:, :], op0=ALU.add, op1=ALU.mult))
            step(v.memset(pmx[:, :], -1.0))
            step(v.memset(cwx[:, :], 0.0))
            for r in range(3):
                dst = pmx[:, :].rearrange("p (t s) -> p t s", t=3)[:, :, NE * r:NE * r + NE]
                v.tensor_scalar(dst, e3(pm), 1.0, float(SLOTS * r), ALU.subtract, ALU.subtract)
                dst = cwx[:, :].rearrange("p (t s) -> p t s", t=3)[:, :, NE * r:NE * r + NE]
                step(v.tensor_copy(dst, e3(cwt)))
            step(v.tensor_reduce(cnt[:, :], ps[7][:, 24:32], AX, ALU.max))
            step(v.tensor_scalar(c_a[:, :], cnt[:, :], float(SLOTS), None, ALU.is_gt))
            step(v.tensor_scalar(cnt[:, :], cnt[:, :], float(2 * SLOTS), None, ALU.is_gt))
            step(v.tensor_tensor(cnt[:, :], cnt[:, :], c_a[:, :], ALU.add))
            v.tensor_scalar(nit[:, :], cnt[:, :], float(NE), float(NE), ALU.mult, ALU.add).then_inc(rounds_ready, 1)
            ve.wait_ge(rounds_ready, 1)
            n_it = ve.value_load(nit[0:1, 0:1], min_val=8, max_val=24)

            def select(e):
                v.tensor_copy(cur[:, 0:3], pmx[:, :].rearrange("p (t s) -> p t s", t=3)[:, :, bass.ds(e, 1)].rearrange("p t s -> p (t s)"))
                v.tensor_copy(cur[:, 3:6], cwx[:, :].rearrange("p (t s) -> p t s", t=3)[:, :, bass.ds(e, 1)].rearrange("p t s -> p (t s)")).then_inc(cur_ready, 1)
                ve.wait_ge(cur_ready, e + 1)
                for t in range(3):
                    ins = v.tensor_scalar(sel[:, t, :], const("iota"), cur[:, t:t + 1], None, ALU.is_equal)
                ins.then_inc(sel_built, 1)

            def mlo(q, i=0):
                ve.wait_ge(mhi_done, i * N_EXP + (q + 1))
                v.tensor_tensor(mwlo[q % MSPLIT][:, :, :], mraw[:, q % MRING, :].rearrange("p (k n) -> p k n", n=512),
                                f32(mwhi[q % MSPLIT][:, :, :]), ALU.subtract).then_inc(mlo_done, 1)

            select(0)
            for q in range(LEAD):
                mlo(q)
            with ve.Fori(0, n_it) as i:
                for j in range(N_EXP):
                    mlo(j + LEAD, i)
                    if j == 4:
                        ve.wait_ge(st_mm, i + 1)
                        select(i + 1)
                    if j in (7, 15, 27):
                        n = (7, 15, 27).index(j)
                        ve.wait_ge(mpe_chunk, i * N_EXP + (j + 1))
                        ve.wait_ge(m_silu, i * 3 + (n + 1))
                        ve.wait_ge(t_mm, i * 3 + n)
                        v.tensor_tensor(eh[:, :], ps[1][:, :], esg[:, :], ALU.mult).then_inc(m_h, 1)
                    if j in (12, 24, 31):
                        n = (12, 24, 31).index(j)
                        ve.wait_ge(ht_hi, i * 3 + (n + 1))
                        v.tensor_tensor(htl[:, :, :], ps[4][:, :].rearrange("p (k n) -> p k n", k=4),
                                        f32(hth[:, :, :]), ALU.subtract).then_inc(ht_lo, 1)
                for h in range(2):
                    ve.wait_ge(ye_hi, i * 2 + (h + 1))
                    v.scalar_tensor_tensor(out=yel[:, 512 * h:512 * h + 512], in0=ps[2 + h][:, :], scalar=cws[:, 0:1],
                                           in1=f32(yeh[:, 512 * h:512 * h + 512]), op0=ALU.mult, op1=ALU.subtract).then_inc(ye_lo, 1)
                for m in range(KD):
                    ve.wait_ge(sc_mm, i * KD + (m + 1))
                    v.tensor_tensor(x[:, m, :], ps[(7, 4)[m % 2]][:, 0:T], x[:, m, :], ALU.add).then_inc(m_add, 1)
            norm(4, split=False)

        @block.tensor
        def _(pe):
            mm = nc.tensor.matmul

            def three(out, wh, wl, xh, xl, start, stop):
                mm(out, wh, xh, start=start, stop=False)
                mm(out, wh, xl, start=False, stop=False)
                return mm(out, wl, xh, start=False, stop=stop)

            def chunk(c, out, xh, xl, i=0, step_=0, start=True, stop=True):
                pe.wait_ge(lo_done, i * step_ + (c + 1))
                for k in range(8):
                    ins = three(out, whi[c % SPLIT][:, k, :], wlo[c % SPLIT][:, k, :], xh[:, k, :], xl[:, k, :],
                                start and k == 0, stop and k == 7)
                ins.then_inc(pe_chunk, 1)

            def norm(n):
                for k in range(KD):
                    pe.wait_ge(sq_done, KD * n + k + 1)
                    ins = mm(ps[7][:, 0:T], ones, sq[:, k, :], start=k == 0, stop=k == KD - 1)
                ins.then_inc(sumsq_done, 1)

            pe.wait_ge(consts_loaded, 48)
            for l in range(2):
                c0, u0 = BASE[l], NU * l
                norm(2 * l)
                pe.wait_ge(xlo_done, 16 * l + KD)
                chunk(c0, ps[0][:, 0:T], xnh, xnl)
                chunk(c0 + 1, ps[1][:, 0:T], xnh, xnl)
                with pe.Fori(0, (N_IN - 2) // 4) as i:
                    for j in range(4):
                        pe.wait_ge(z_evac, i * 4 + (N_IN * l + j + 1))
                        chunk(c0 + 2 + j, ps[j % 2][:, 0:T], xnh, xnl, i, 4)

                for j in range(N_G):
                    c = c0 + N_IN + j
                    half, part, pair = j // 4, j % 2, j // 2
                    pe.wait_ge(lo_done, c + 1)
                    slot = 0
                    for i in ((3, 4) if part else (0, 1, 2)):
                        pe.wait_ge(xc_split, KR * l + 5 * half + GATE_IN[i][-1] + 1)
                        if pair:
                            pe.wait_ge(gate_evac, 20 * l + 5 * (pair - 1) + i + 1)
                        for k in GATE_IN[i]:
                            t = 5 * half + k
                            ins = three(ps[2 + i][:, 0:C], whi[c % 2][:, slot, :], wlo[c % 2][:, slot, :], xch[:, t, :],
                                        xcl[:, t, :], k == GATE_IN[i][0], k == GATE_IN[i][-1])
                            slot += 1
                    ins.then_inc(pe_chunk, 1)

                pe.wait_ge(z_evac, N_IN * (l + 1))
                vt = qkx[:, 9, :]
                for t in range(3):
                    a, b = 128 * t, min(128 * t + 128, TP)
                    nc.tensor.transpose(ps[0][0:b - a, 128 * t:128 * t + 128], vt[:, a:b], ident)
                for b in range(SB):
                    ins = nc.tensor.transpose(ps[(1, 7)[b // 4]][0:SS, 128 * (b % 4):128 * (b % 4) + 128],
                                              vt[:, TP + SS * b:TP + SS * b + SS], ident)
                ins.then_inc(vt_mm, 1)
                pe.wait_ge(gate_evac, 20 * (l + 1))
                pe.wait_ge(k_ready, l + 1)
                pe.wait_ge(qt_ready, l + 1)

                def scores(u):
                    kind, k = ATT_UNITS[u]
                    if u >= 2:
                        pe.wait_ge(s_neg, u0 + u - 1)
                    for i in range(2):
                        for g in range(2):
                            r = slice(64 * g, 64 * g + 64)
                            bank = ps[2 + 2 * (u % 2) + g]
                            if kind == "A":
                                ins = mm(bank[:, 128 * i:128 * i + 128], qkx[r, 2 * k + i, 0:128], qkx[r, 8, 0:128], start=True, stop=True)
                            elif kind == "D":
                                b = 2 * k + i
                                w = ATT_W["D"]
                                ins = mm(bank[r, w * i:w * i + w], qt[r, 128 + 64 * b:192 + 64 * b], kc[r, b, :], start=True, stop=True)
                            elif i == 0 and kind == "B":
                                ins = mm(bank[:, 0:256], qkx[r, k, 128:256], qkx[r, 8, 0:256], start=True, stop=True)
                            elif i == 0:
                                ins = mm(bank[:, 0:144], qt[r, 0:128], qkx[r, 8, 128:TP], start=True, stop=True)
                    ins.then_inc(s_mm, 1)

                def turn(u):
                    kind, _ = ATT_UNITS[u]
                    q, w = u % 2, ATT_W[kind]
                    pe.wait_ge(p_norm, u0 + u + 1)
                    if u >= 2:
                        pe.wait_ge(pt_copied, 2 * (u0 + u - 1))
                    for s in range(4):
                        if kind in "AB":
                            out, src = ps[6 + q][:, 128 * s:128 * s + 128], sp[q][:, 128 * s:128 * s + 128]
                        else:
                            n = P if s < 2 else w - P
                            a = w * (s % 2) + (0 if s < 2 else P)
                            out, src = ps[6 + q][0:n, 128 * s:128 * s + 128], sp[q][:, a:a + n]
                        ins = nc.tensor.transpose(out, src, ident)
                    ins.then_inc(pt_mm, 1)

                def values(u):
                    kind, k = ATT_UNITS[u]
                    q = u % 2
                    pe.wait_ge(pt_copied, 2 * (u0 + u + 1))
                    if u >= 2:
                        pe.wait_ge(o_lo, u0 + u - 1)
                    for g in range(2):
                        r = slice(64 * g, 64 * g + 64)
                        if kind == "A":
                            for i in range(2):
                                ins = mm(ps[q][r, 128 * i:128 * i + 128], vp[:, 0, r], pt[q][:, 2 * g + i, :], start=True, stop=True)
                        elif kind == "B":
                            for t in range(2):
                                ins = mm(ps[q][r, 0:128], vp[:, t, r], pt[q][:, 2 * g + t, :], start=t == 0, stop=t == 1)
                        elif kind == "C":
                            few = TP - 256
                            mm(ps[q][r, 0:128], vp[:, 1, r], pt[q][:, g, :], start=True, stop=False)
                            ins = mm(ps[q][r, 0:128], vp[0:few, 2, r], pt[q][0:few, 2 + g, :], start=False, stop=True)
                        else:
                            for i in range(2):
                                b = 2 * k + i
                                out = ps[q][r, 0:128].rearrange("p (h i s) -> p h i s", i=2, s=SS)[:, :, i, :]
                                mm(out, vc[:, b, r], pt[q][:, i, r], start=True, stop=False)
                                ins = mm(out, vnew[:, b, r], pt[q][0:SS, 2 + i, r], start=False, stop=True)
                    ins.then_inc(pv_mm, 1)

                scores(0)
                pe.wait_ge(v_ready, 4 * (l + 1))
                pe.wait_ge(vcache_loaded, 16 * (l + 1))
                for s in range(NU + 1):
                    if s + 1 < NU:
                        scores(s + 1)
                    if s < NU:
                        turn(s)
                    if s >= 1:
                        values(s - 1)

                pe.wait_ge(o_lo, NU * (l + 1))
                for m in range(N_A):
                    if m >= 2:
                        pe.wait_ge(ap_post, KD * l + m - 1)
                    chunk(c0 + 54 + m, ps[m % 2][:, 0:T], atth, attl)

                pe.wait_ge(rec_split, l + 1)
                pe.wait_ge(ap_post, KD * (l + 1))
                for n in range(KD * KR):
                    m, k, c = n // KR, n % KR, c0 + 62 + n // 8
                    if n % 8 == 0:
                        pe.wait_ge(lo_done, c + 1)
                    if k == 0 and m >= 2:
                        pe.wait_ge(rp_post, KD * l + m - 1)
                    ins = three(ps[m % 2][:, 0:T], whi[c % 2][:, n % 8, :], wlo[c % 2][:, n % 8, :], rech[:, k, :],
                                recl[:, k, :], k == 0, k == KR - 1)
                    if n % 8 == 7:
                        ins.then_inc(pe_chunk, 1)

                pe.wait_ge(mg_split, KD * (l + 1))
                for m in range(N_O):
                    if m >= 2:
                        pe.wait_ge(x_added, 16 * l + m - 1)
                    chunk(c0 + 72 + m, ps[m % 2][:, 0:T], mgh, mgl)
                norm(2 * l + 1)

                if l == 0:
                    f0 = N_MIX
                    pe.wait_ge(xlo_done, 2 * KD)

                    def gate_up(m, i=0):
                        q = m % 2
                        if m >= 2:
                            pe.wait_ge(ffn_silu, i * 2 + (m - 1))
                        chunk(f0 + 2 * m, ps[2 * q][:, 0:T], xnh, xnl, i, 4)
                        if m >= 2:
                            pe.wait_ge(ffn_h, i * 2 + (m - 1))
                        chunk(f0 + 2 * m + 1, ps[2 * q + 1][:, 0:T], xnh, xnl, i, 4)

                    gate_up(0)
                    gate_up(1)
                    with pe.Fori(0, KF // 2 - 1) as i:
                        gate_up(2, i)
                        gate_up(3, i)
                    pe.wait_ge(ffn_lo, KF)
                    with pe.Fori(0, 2) as i:
                        for j in range(12):
                            m, third = j // 3, j % 3
                            if third == 0:
                                pe.wait_ge(x_added, i * 4 + (KD + m - 1))
                            chunk(f0 + 2 * KF + j, ps[4 + m % 2][:, 0:T], hfh[:, 8 * third:8 * third + 8, :],
                                  hfl[:, 8 * third:8 * third + 8, :], i, 12, third == 0, third == 2)

            pe.wait_ge(nt_done, 4 * KD)
            for t, (a, rows) in enumerate(TT):
                for f in range(2):
                    for k in range(4):
                        ins = nc.tensor.transpose(ps[2 * t + f][0:rows, 128 * k:128 * k + 128], nt[:, 4 * f + k, a:a + rows], ident)
                    ins.then_inc(tok_mm, 1)
            for t, (a, rows) in enumerate(TT):
                for k in range(KD):
                    ins = mm(ps[6][0:rows, NE * t:NE * t + NE], nt[:, k, a:a + rows], wrt[:, NE * k:NE * k + NE], start=k == 0, stop=k == KD - 1)
            ins.then_inc(router_mm, 1)
            pe.wait_ge(mask_ready, 1)
            for t in range(3):
                for s in range(t + 1):
                    mm(ps[7][:, NE * t:NE * t + NE], const("tri") if s == t else ones, msk[:, NE * s:NE * s + NE], start=s == 0, stop=s == t)
            for s in range(3):
                ins = mm(ps[7][:, 24:32], ones, msk[:, NE * s:NE * s + NE], start=s == 0, stop=s == 2)
            ins.then_inc(pos_mm, 1)
            pe.wait_ge(rounds_ready, 1)
            n_it = pe.value_load(nit[0:1, 0:1], min_val=8, max_val=24)

            def gather(f, e):
                src = (tokh, tokl)[f // 2]
                for k in range(4):
                    for t, (_, rows) in enumerate(TT):
                        col = P * (4 * (f % 2) + k)
                        ins = mm(ps[5 + f % 2][:, 128 * k:128 * k + 128], src[0:rows, t, col:col + P], sel[0:rows, t, :],
                                 start=t == 0, stop=t == 2)
                ins.then_inc(g_mm, 1)

            def selt_and_weights():
                for t, (a, rows) in enumerate(TT):
                    nc.tensor.transpose(ps[7][:, a:a + rows], sel[0:rows, t, :].bitcast(F32), ident[0:rows, 0:rows])
                for t, (a, rows) in enumerate(TT):
                    ins = mm(ps[7][:, 340:341], sel[0:rows, t, :].bitcast(F32), cur[0:rows, 3 + t:4 + t], start=t == 0, stop=t == 2)
                ins.then_inc(st_mm, 1)

            def expert_chunk(j, i, lhs_h, lhs_l, outs, start, stop):
                pe.wait_ge(mlo_done, i * N_EXP + (j + 1))
                s = j % MSPLIT
                for n in range(2):
                    mm(outs[n], lhs_h[n], mwhi[s][:, n, :], start=start[n], stop=False)
                    mm(outs[n], lhs_h[n], mwlo[s][:, n, :], start=False, stop=False)
                    ins = mm(outs[n], lhs_l[n], mwhi[s][:, n, :], start=False, stop=stop[n])
                ins.then_inc(mpe_chunk, 1)

            pe.wait_ge(tok_lo, 6)
            pe.wait_ge(sel_built, 1)
            for f in range(4):
                if f >= 2:
                    pe.wait_ge(g_evac, f - 1)
                gather(f, 0)
            selt_and_weights()
            with pe.Fori(0, n_it) as i:
                def into(j0, bank, ready, count):
                    pe.wait_ge(ready, count)
                    for d in range(4):
                        k = 2 * d
                        expert_chunk(j0 + d, i, [xeh[:, k, :], xeh[:, k + 1, :]], [xel[:, k, :], xel[:, k + 1, :]],
                                     [ps[bank][:, :]] * 2, [d == 0, False], [False, d == 3])

                def turn_hidden(n):
                    pe.wait_ge(m_h, i * 3 + (n + 1))
                    if n == 0:
                        pe.wait_ge(m_add, i * KD)
                    else:
                        pe.wait_ge(ht_lo, i * 3 + n)
                    for k in range(4):
                        ins = nc.tensor.transpose(ps[4][:, 128 * k:128 * k + 128], eh[:, 128 * k:128 * k + 128], ident)
                    ins.then_inc(t_mm, 1)

                def down(j0, n):
                    pe.wait_ge(ht_lo, i * 3 + (n + 1))
                    if n == 0:
                        pe.wait_ge(ye_lo, i * 2)
                    for d in range(4):
                        expert_chunk(j0 + d, i, [hth[:, d, :]] * 2, [htl[:, d, :]] * 2, [ps[2][:, :], ps[3][:, :]],
                                     [n == 0 and d == 0] * 2, [n == 2 and d == 3] * 2)

                pe.wait_ge(g_evac, i * 4 + 4)
                into(0, 0, m_silu, i * 3)
                into(4, 1, m_h, i * 3)
                into(8, 0, m_silu, i * 3 + 1)
                turn_hidden(0)
                into(12, 1, m_h, i * 3 + 1)
                down(16, 0)
                into(20, 0, m_silu, i * 3 + 2)
                turn_hidden(1)
                into(24, 1, m_h, i * 3 + 2)
                down(28, 1)
                turn_hidden(2)
                pe.wait_ge(sel_built, i + 2)
                gather(0, i + 1)
                gather(1, i + 1)
                down(32, 2)
                pe.wait_ge(g_evac, i * 4 + 5)
                gather(2, i + 1)
                pe.wait_ge(g_evac, i * 4 + 6)
                gather(3, i + 1)
                pe.wait_ge(ye_lo, i * 2 + 2)
                for m in range(KD):
                    if m >= 2:
                        pe.wait_ge(m_add, i * KD + (m - 1))
                    out = ps[(7, 4)[m % 2]][:, 0:T]
                    mm(out, yeh[:, P * m:P * m + P], selt[:, :], start=True, stop=False)
                    mm(out, yel[:, P * m:P * m + P], selt[:, :], start=False, stop=True).then_inc(sc_mm, 1)
                pe.wait_ge(m_add, i * KD + 7)
                selt_and_weights()
            norm(4)


def kernel(**inputs):
    import concourse.bacc as bacc
    from concourse.bass_utils import run_bass_kernel_spmd

    f = {k: np.asarray(v) for k, v in inputs.items()}

    def cols(a):
        a = a.reshape(*a.shape[:-1], -1, P)
        return np.moveaxis(a, -1, 0)

    def chunks(w):
        k, m = w.shape
        t = w.reshape(k // P, P, m // P, P).transpose(2, 0, 1, 3).reshape(-1, 8, P, P)
        return t.transpose(0, 2, 1, 3).reshape(-1, P, CH)

    heads = np.arange(1024).reshape(2, 8, HD).transpose(1, 0, 2).reshape(-1)
    o = np.cumsum([0, 1024, 128, 128, REC, REC, D, D])
    order = np.concatenate([heads, np.arange(o[1], o[3]), np.arange(o[3], o[4]), np.arange(o[5], o[7]), np.arange(o[4], o[5])])

    def gate_chunks(wa, wi):
        full = []
        for w in (wa, wi):
            z = np.zeros((REC, REC), w.dtype)
            for n in range(16):
                z[80 * n:80 * n + 80, 80 * n:80 * n + 80] = w[n]
            full.append(z)
        out = np.zeros((N_G, P, 8, P), wa.dtype)
        for j in range(N_G):
            half, gate, part = j // 4, j // 2 % 2, j % 2
            slot = 0
            for i in ((3, 4) if part else (0, 1, 2)):
                for k in GATE_IN[i]:
                    a, b = P * (5 * half + k), P * (5 * half + i)
                    out[j, :, slot, :] = full[gate][a:a + P, b:b + P]
                    slot += 1
        return out.reshape(N_G, P, CH)

    w_mix = np.stack([np.concatenate([
        chunks(f["w_in"][l][:, order]), gate_chunks(f["w_rg_a"][l], f["w_rg_i"][l]), chunks(f["w_att_proj"][l][heads]),
        chunks(f["w_rec_proj"][l]), chunks(f["w_out"][l])]) for l in range(2)])
    gu = np.stack([chunks(f["w_ffn_gate"][0]), chunks(f["w_ffn_up"][0])], 1).reshape(-1, P, CH)
    w_ffn = np.concatenate([gu, chunks(f["w_ffn_down"][0])])

    def wide(w, n):
        t = w[:, 512 * n:512 * n + 512].reshape(-1, 2, P, 512)
        return t.transpose(0, 2, 1, 3).reshape(-1, P, CH)

    def down(w, n):
        return w[512 * n:512 * n + 512].reshape(4, P, CH)

    moe = []
    for e in range(NE):
        g, u, d = f["w_exp_gate"][0, e], f["w_exp_up"][0, e], f["w_exp_down"][0, e]
        moe += [wide(g, 0), wide(u, 0), wide(g, 1), wide(u, 1), down(d, 0), wide(g, 2), wide(u, 2), down(d, 1), down(d, 2)]
    moe.append(moe[0][:4])
    moe += [moe[1][:4], moe[2][:1]]
    w_moe = np.concatenate(moe)

    tokens = np.concatenate([f["meta_tokens"], f["x_prompt"][0], f["x_sample"].reshape(TS, D)])
    x_in = cols(tokens).transpose(0, 2, 1)

    p = np.arange(P)[:, None]

    def mask(s, w):
        i = np.arange(w)[None, :]
        return np.where((i >= s) & (i <= s + WIN), 0.0, -1e30)

    m_a = np.where(np.arange(128)[None, :] <= p, 0.0, -1e30)
    consts = np.concatenate([
        np.eye(P), np.ones((P, P)), np.tile(m_a, (1, 2)), mask(p, 256), mask(p % 16, 144), mask(p % 8, 136),
        (p < np.arange(P)[None, :]) * 1.0, np.broadcast_to(np.arange(SLOTS), (P, SLOTS)),
        np.broadcast_to(np.tile(NE - np.arange(NE), 3), (P, 24)),
        (p + 128 * np.repeat(np.arange(3), NE)[None, :] < T) * 1.0], axis=1).astype(np.float32)

    def sinks(s):
        s = s.reshape(2, 8)
        a = s.reshape(2, 4, 2).transpose(1, 0, 2).reshape(1, 16)
        b = s.T.reshape(1, 16)
        c = np.repeat(s, 16, axis=1).T
        d = np.repeat(s.reshape(-1), 8)[:, None]
        return np.concatenate([np.broadcast_to(a, (P, 16)), np.broadcast_to(b, (P, 16)), c, d, d], axis=1)

    par = np.stack([np.concatenate([
        cols(f["ln_mix"][l]), cols(f["ln_ffn"][l]), cols(f["w_conv"][l]).reshape(P, -1), cols(f["b_conv"][l]),
        cols(f["b_rg_a"][l]), cols(f["b_rg_i"][l]), cols(f["rg_lambda"][l]), sinks(f["attn_sinks"][l])], axis=1)
        for l in range(2)], axis=1)
    misc = np.concatenate([cols(f["ln_final"]), f["w_router"][0].reshape(KD, P, NE).transpose(1, 0, 2).reshape(P, -1),
                           np.broadcast_to(np.tile(f["b_router"][0], 3), (P, 24))], axis=1)
    state = np.stack([np.concatenate([
        cols(f["state_conv"][l]).transpose(0, 3, 1, 2).reshape(P, -1),
        cols(f["state_rglru"][l]).transpose(0, 2, 1).reshape(P, -1)], axis=1) for l in range(2)])
    kc = f["cache_k"].reshape(2, SB, WIN, P).transpose(0, 3, 1, 2)
    vc = f["cache_v"].reshape(2, SB, WIN, P).transpose(0, 2, 1, 3)

    ins = {"w_mix": w_mix, "w_ffn": w_ffn, "w_moe": w_moe, "x_in": x_in, "consts_in": consts, "par_in": par,
           "misc_in": misc, "state_in": state, "kc_in": kc, "vc_in": vc}
    outs = {"o_y": (P, KD, T), "o_kp": (2, P, WIN), "o_vp": (2, P, WIN), "o_ks": (2, P, SB, WIN),
            "o_vs": (2, WIN, SB, P), "o_state": (2, P, STATE_OUT)}
    nc = bacc.Bacc("TRN2", target_bir_lowering=False, num_devices=1)
    arrays = {k: np.ascontiguousarray(a) for k, a in ins.items()}
    args = [nc.dram_tensor(k, a.shape, F32, kind="ExternalInput").ap() for k, a in arrays.items()]
    args += [nc.dram_tensor(k, s, F32, kind="ExternalOutput").ap() for k, s in outs.items()]
    build_step(nc, *args)
    got = run_bass_kernel_spmd(nc, [arrays], core_ids=[0]).results[0]

    y = got["o_y"].transpose(2, 1, 0).reshape(T, D)
    st = got["o_state"]

    def rows(a, k):
        return a.reshape(2, P, KR, k).transpose(0, 3, 2, 1).reshape(2, k, REC)

    def kv(a):
        return a.transpose(0, 2, 1).reshape(2, 1, WIN, 2, HD)

    return (np.ascontiguousarray(y[META:TP])[None], np.ascontiguousarray(y[TP:]).reshape(SB, SS, D),
            kv(got["o_kp"]), kv(got["o_vp"]), rows(st[:, :, 0:30], 3)[:, None], rows(st[:, :, 270:280], 1),
            np.ascontiguousarray(got["o_ks"].transpose(0, 2, 3, 1)).reshape(2, SB, WIN, 2, HD),
            np.ascontiguousarray(got["o_vs"].transpose(0, 2, 1, 3)).reshape(2, SB, WIN, 2, HD),
            rows(st[:, :, 30:270], 24).reshape(2, SB, 3, REC), rows(st[:, :, 280:360], 8))
```

```python
from contextlib import ExitStack

import numpy as np

import concourse.bass as bass
from concourse import mybir

F32 = mybir.dt.float32
F32R = mybir.dt.float32r
I32 = mybir.dt.int32
ALU = mybir.AluOpType
ACT = mybir.ActivationFunctionType
AX = mybir.AxisListType.X

P = 128
D = 1024
KD = D // P
META, SEQ, SB, SS = 16, 256, 8, 8
TP = META + SEQ
TS = SB * SS
T = TP + TS
WIN = 128
HD = 64
REC = 1280
KR = REC // P
CW = 4
EP = CW - 1 + SS
EXT = CW - 1 + TP + SB * EP
C = EXT - (CW - 1)
FF = 3072
KF = FF // P
EFF = 1536
NE = 8
SLOTS = 128
EPS = 1e-6
BASE_ADDR = 16512
TT = [(0, 128), (128, 128), (256, T - 256)]

CH = 8 * P
N_IN = 46
N_G, N_A, N_R, N_O = 8, 8, 10, 8
N_Q, N_MG = 20, 16
C_G = N_Q + N_MG
C_Y = C_G + N_G
C_A = C_Y + KR
C_R = C_A + N_A
C_O = C_R + N_R
N_MIX = N_IN + N_G + N_A + N_R + N_O
N_FFN = 3 * KF
N_EXP = 36
N_MOE = NE * N_EXP
BASE = [0, N_MIX + N_FFN]
RING, SPLIT = 4, 2
MRING, MSPLIT, LEAD = 9, 4, 3

ATT_UNITS = [("A", u) for u in range(4)] + [("B", u) for u in range(8)] + [("C", 0)] + [("D", u) for u in range(4)]
NU = len(ATT_UNITS)
ATT_W = {"A": 128, "B": 256, "C": 144, "D": 136}
ATT_N = {"A": 4, "B": 2, "C": 2, "D": 2}
SINK0 = {"A": 0, "B": 16, "C": 32, "D": 34}

CONST_SIZES = [("ident", 128), ("ones", 128), ("mA", 256), ("mB", 256), ("mC", 144), ("mD", 136),
               ("tri", 128), ("iota", 128), ("rank", 24), ("valid", 24)]
PAR_SIZES = [("ln_mix", 8), ("ln_ffn", 8), ("w_conv", 40), ("b_conv", 10), ("b_a", 10), ("b_i", 10),
             ("lam", 10), ("sinks", 36)]


def offsets(sizes):
    out, at = {}, 0
    for name, n in sizes:
        out[name] = (at, at + n)
        at += n
    return out, at


CONST, N_CONST = offsets(CONST_SIZES)
PAR, N_PAR = offsets(PAR_SIZES)
GATE_IN = [[0, 1], [0, 1, 2], [1, 2, 3], [2, 3, 4], [3, 4]]
STATE_IN = KR * (SB * 3 + SB)
STATE_OUT = KR * (3 + SB * 3 + 1 + SB)


def build_step(nc, w_mix, w_ffn, w_moe, x_in, consts_in, par_in, misc_in, state_in, kc_in, vc_in,
               o_y, o_kp, o_vp, o_ks, o_vs, o_state):
    with ExitStack() as ctx:
        slab = ctx.enter_context(nc.sbuf_tensor("slab", [P, 212800 // 4], F32))
        base = BASE_ADDR
        used = {}

        def at(name, shape, dt, off):
            n = int(np.prod(shape[1:])) * 4
            assert off + n <= 212800, (name, off + n)
            used[name] = (off, off + n)
            return nc.alloc_sbuf_tensor_at(name, shape, dt, offset=base + off)

        x = at("x", [P, KD, T], F32, 0)
        raw = at("raw", [P, RING, CH], F32, 10752)
        whi = [at(f"whi{i}", [P, 8, P], F32R, 27136 + 8192 * i) for i in range(SPLIT)]
        wlo = [at(f"wlo{i}", [P, 8, P], F32R, 31232 + 8192 * i) for i in range(SPLIT)]
        xnh = at("xnh", [P, KD, T], F32R, 43520)
        xnl = at("xnl", [P, KD, T], F32R, 54272)
        atth = at("atth", [P, KD, T], F32R, 43520)
        attl = at("attl", [P, KD, T], F32R, 54272)
        qkx = at("qkx", [P, 20, T], F32, 65024)
        gates = at("gates", [P, 16, T], F32, 92864)
        yr = at("yr", [P, KR, T], F32, 114368)
        R_, E_, XC_, I_ = 127808, 142208, 156736, 171136
        rg = at("rg", [P, KR, C], F32, R_)
        ext = at("ext", [P, KR, EXT], F32, E_)
        xc = at("xc", [P, KR, C], F32, XC_)
        ig = at("ig", [P, KR, C], F32, I_)
        xch = at("xch", [P, KR, C], F32R, 78464)
        xcl = at("xcl", [P, KR, C], F32R, E_)
        vnew = at("vnew", [SS, SB, P], F32, I_)
        sp = [at(f"sp{i}", [P, 512], F32, I_ + 4096 + 2048 * i) for i in range(2)]
        pt = [at(f"pt{i}", [P, 4, P], F32, I_ + 8192 + 2048 * i) for i in range(2)]
        asq = at("asq", [P, KR, C], F32, E_)
        mul = at("mul", [P, KR, C], F32, 78464)
        hs = at("hs", [P, KR, C], F32, XC_)
        rect = at("rect", [P, KR, T], F32, I_)
        rech = at("rech", [P, KR, T], F32R, E_)
        recl = at("recl", [P, KR, T], F32R, 78464)
        mgh = at("mgh", [P, KD, T], F32R, R_)
        mgl = at("mgl", [P, KD, T], F32R, XC_)
        sq = at("sq", [P, KD, T], F32, I_)
        nt = at("nt", [P, KD, T], F32, E_)
        rms = at("rms", [P, T], F32, E_ + 10752)
        rstd = at("rstd", [P, T], F32, E_ + 12096)
        hfh = at("hfh", [P, KF, T], F32R, 65024)
        hfl = at("hfl", [P, KF, T], F32R, 97280)
        sg = [at(f"sg{i}", [P, T], F32, XC_ + 1344 * i) for i in range(2)]
        hh = at("hh", [P, T], F32, XC_ + 2688)
        tokh = at("tokh", [P, 3, D], F32R, 43520)
        tokl = at("tokl", [P, 3, D], F32R, 55808)
        mwhi = [at(f"mwhi{i}", [P, 2, 512], F32R, 68096 + 8192 * i) for i in range(MSPLIT)]
        mwlo = [at(f"mwlo{i}", [P, 2, 512], F32R, 72192 + 8192 * i) for i in range(MSPLIT)]
        mraw = at("mraw", [P, MRING, CH], F32, 100864)
        xeh = at("xeh", [P, KD, SLOTS], F32R, 10752)
        xel = at("xel", [P, KD, SLOTS], F32R, 14848)
        eh = at("eh", [P, 512], F32, 18944)
        esg = at("esg", [P, 512], F32, 20992)
        yeh = at("yeh", [P, D], F32R, 23040)
        yel = at("yel", [P, D], F32R, 27136)
        hth = at("hth", [P, 4, SLOTS], F32R, 31232)
        htl = at("htl", [P, 4, SLOTS], F32R, 33280)
        sel = at("sel", [P, 3, SLOTS], F32R, 35328)
        selt = at("selt", [P, T], F32R, 36864)
        o = 185536
        kc = at("kc", [P, SB, WIN + SS], F32, o); o += 4352
        vc = at("vc", [P, SB, P], F32, o); o += 4096
        vp = at("vp", [P, 3, P], F32, o); o += 1536
        cst = at("cst", [P, N_CONST], F32, o); o += (N_CONST * 4 + 31) // 32 * 32
        par = at("par", [P, 2, N_PAR], F32, o); o += (2 * N_PAR * 4 + 31) // 32 * 32
        misc = at("misc", [P, 8 + 64 + 24], F32, o); o += 384
        stin = at("stin", [P, STATE_IN], F32, o); o += STATE_IN * 4
        stout = at("stout", [P, STATE_OUT], F32, o); o += STATE_OUT * 4

        qt = at("qt", [P, (TP - 256 + TS) * 8], F32, o); o += 2560

        def small(name, n, dt=F32):
            nonlocal o
            t = at(name, [P, n], dt, o)
            o += (n * 4 + 31) // 32 * 32
            return t

        c1 = small("c1", 20); c2 = small("c2", 20); cm = small("cm", 20)
        sp_e = small("sp_e", 20); sp_z = small("sp_z", 20); sp_p = small("sp_p", 20); sp_q = small("sp_q", 20)
        nsink = small("nsink", 72)
        eps = small("eps", 1)
        mx = [small(f"mx{i}", 4) for i in range(2)]
        neg = [small(f"neg{i}", 4) for i in range(2)]
        dsk = [small(f"dsk{i}", 4) for i in range(2)]
        esk = [small(f"esk{i}", 4) for i in range(2)]
        rsum = [small(f"rsum{i}", 4) for i in range(2)]
        rinv = [small(f"rinv{i}", 4) for i in range(2)]
        lg = small("lg", 24); lg2 = small("lg2", 24); eq = small("eq", 24); oh1 = small("oh1", 24)
        oh2 = small("oh2", 24); top1 = small("top1", 3); top2 = small("top2", 3); rk = small("rk", 3)
        dlt = small("dlt", 3); e2 = small("e2", 3); w1 = small("w1", 3); w2 = small("w2", 3)
        msk = small("msk", 24); cwt = small("cwt", 24); pm = small("pm", 24)
        pmx = small("pmx", 3 * 25); cwx = small("cwx", 3 * 25)
        cur = small("cur", 6); cws = small("cws", 1); cnt = small("cnt", 1); c_a = small("c_a", 1)
        nit = small("nit", 1, I32)

        ps = [ctx.enter_context(nc.psum_tensor(f"ps{i}", [P, 512], F32)) for i in range(8)]

        def sem(name):
            return ctx.enter_context(nc.semaphore(name))

        consts_loaded, x_loaded = sem("consts_loaded"), sem("x_loaded")
        raw_loaded = [sem(f"raw_loaded{i}") for i in range(RING)]
        mraw_loaded = [sem(f"mraw_loaded{i}") for i in range(MRING)]
        hi_done, lo_done, pe_chunk = sem("hi_done"), sem("lo_done"), sem("pe_chunk")
        mhi_done, mlo_done, mpe_chunk = sem("mhi_done"), sem("mlo_done"), sem("mpe_chunk")
        sq_done, sumsq_done, rms_done = sem("sq_done"), sem("sumsq_done"), sem("rms_done")
        nt_done, xhi_done, xlo_done = sem("nt_done"), sem("xhi_done"), sem("xlo_done")
        x_added, z_evac = sem("x_added"), sem("z_evac")
        ext_history, ext_ready, conv_saved, xc_split = sem("ext_history"), sem("ext_ready"), sem("conv_saved"), sem("xc_split")
        gate_evac = sem("gate_evac")
        kcache_loaded, vcache_loaded, state_loaded = sem("kcache_loaded"), sem("vcache_loaded"), sem("state_loaded")
        qt_ready = sem("qt_ready")
        k_ready, vt_mm, v_ready = sem("k_ready"), sem("vt_mm"), sem("v_ready")
        yr_ready, gates_ready = sem("yr_ready"), sem("gates_ready")
        s_mm, s_neg, p_exp, p_norm = sem("s_mm"), sem("s_neg"), sem("p_exp"), sem("p_norm")
        pt_mm, pt_copied, pv_mm, o_evac = sem("pt_mm"), sem("pt_copied"), sem("pv_mm"), sem("o_evac")
        att_hi, att_lo = sem("att_hi"), sem("att_lo")
        ap_post, rp_post, mg_split = sem("ap_post"), sem("rp_post"), sem("mg_split")
        lru_pair, m2_done, m_sqrt = sem("lru_pair"), sem("m2_done"), sem("m_sqrt")
        h_saved = sem("h_saved")
        rec_ready, rec_hi, rec_split = sem("rec_ready"), sem("rec_hi"), sem("rec_split")
        ffn_silu, ffn_h, ffn_hi, ffn_lo = sem("ffn_silu"), sem("ffn_h"), sem("ffn_hi"), sem("ffn_lo")
        act_step, dve_step = sem("act_step"), sem("dve_step")
        c_ready, sp_exp = sem("c_ready"), sem("sp_exp")
        tok_mm, tok_hi, tok_lo = sem("tok_mm"), sem("tok_hi"), sem("tok_lo")
        router_mm, top_gap, top_exp, mask_ready = sem("router_mm"), sem("top_gap"), sem("top_exp"), sem("mask_ready")
        pos_mm, rounds_ready = sem("pos_mm"), sem("rounds_ready")
        cur_ready = sem("cur_ready")
        sel_built, g_mm, g_evac, st_mm, st_evac = sem("sel_built"), sem("g_mm"), sem("g_evac"), sem("st_mm"), sem("st_evac")
        m_silu, m_h, t_mm, ht_hi, ht_lo = sem("m_silu"), sem("m_h"), sem("t_mm"), sem("ht_hi"), sem("ht_lo")
        ye_hi, ye_lo, sc_mm, m_add = sem("ye_hi"), sem("ye_lo"), sem("sc_mm"), sem("m_add")
        out_done, kv_out_done, state_out_done = sem("out_done"), sem("kv_out_done"), sem("state_out_done")

        def const(name):
            a, b = CONST[name]
            return cst[:, a:b]

        ident, ones = const("ident"), const("ones")

        def p_(l, name):
            a, b = PAR[name]
            return par[:, l, a:b]

        lnf, wrt, brt = misc[:, 0:8], misc[:, 8:72], misc[:, 72:96]

        def seqs(t):
            end = t.shape[2]
            return t[:, :, end - SB * EP:end].rearrange("p k (b e) -> p k b e", e=EP)

        def gain(n):
            return lnf if n == 4 else p_(n // 2, "ln_ffn" if n % 2 else "ln_mix")

        def att_part(u):
            kind, i = ATT_UNITS[u]
            o = ps[7]
            if kind == "A":
                return qkx[:, 2 * i:2 * i + 2, 0:P], o[:, 0:256].rearrange("p (k n) -> p k n", k=2)
            if kind == "B":
                return qkx[:, i, P:2 * P], o[:, 0:P]
            first = 2 * P if kind == "C" else TP + 16 * i
            return qkx[:, 0:KD, first:first + 16], o[:, 0:P].rearrange("p (h s) -> p h s", h=KD)

        block = ctx.enter_context(nc.Block())

        @block.sync
        def _(sy):
            sy.dma_start(x[:, :, :], x_in).then_inc(x_loaded, 16)
            sy.dma_start(cst[:, :], consts_in).then_inc(consts_loaded, 16)
            sy.dma_start(par[:, :, :], par_in).then_inc(consts_loaded, 16)
            sy.dma_start(misc[:, :], misc_in).then_inc(consts_loaded, 16)

            def stream(src, c0, n):
                first = 0
                if c0 == 0:
                    for j in range(RING):
                        sy.dma_start(raw[:, j, :], src[j]).then_inc(raw_loaded[j], 16)
                    first = RING
                with sy.Fori(first // 4, n // 4) as i:
                    for j in range(4):
                        sy.wait_ge(lo_done, i * 4 + (c0 + j + 1 - RING))
                        sy.dma_start(raw[:, (c0 + j) % RING, :], src[i * 4 + j]).then_inc(raw_loaded[(c0 + j) % RING], 16)

            stream(w_mix[0], 0, N_MIX)
            stream(w_ffn, N_MIX, N_FFN)
            stream(w_mix[1], BASE[1], N_MIX)
            sy.wait_ge(pe_chunk, BASE[1] + N_MIX)
            for j in range(MRING):
                sy.dma_start(mraw[:, j, :], w_moe[j]).then_inc(mraw_loaded[j], 16)
            sy.wait_ge(rounds_ready, 1)
            n_round = sy.value_load(nit[0:1, 0:1], min_val=8, max_val=24) // NE
            with sy.Fori(0, n_round) as r:
                with sy.Fori(0, N_MOE // MRING) as i:
                    for j in range(MRING):
                        sy.wait_ge(mlo_done, r * N_MOE + i * MRING + (j + 1))
                        sy.dma_start(mraw[:, j, :], w_moe[i * MRING + (MRING + j)]).then_inc(mraw_loaded[j], 16)
            for j in range(MRING):
                sy.wait_ge(mraw_loaded[j], n_round * (16 * N_MOE // MRING) + 16)
            for k in range(KD):
                sy.wait_ge(nt_done, 4 * KD + k + 1)
                sy.dma_start(o_y[:, k, :], nt[:, k, :]).then_inc(out_done, 16)
            sy.wait_ge(out_done, 16 * KD)

        @block.gpsimd
        def _(pool):
            for l in range(2):
                z0 = N_IN * l
                if l == 1:
                    pool.wait_ge(kv_out_done, 16 * 5)
                    pool.wait_ge(pv_mm, NU)
                pool.dma_start(kc[:, :, 0:WIN], kc_in[l]).then_inc(kcache_loaded, 16)
                pool.dma_start(vc[:, :, :], vc_in[l]).then_inc(vcache_loaded, 16)
                pool.dma_start(stin[:, :], state_in[l]).then_inc(state_loaded, 16)
                pool.wait_ge(xlo_done, 16 * l + 8)
                pool.wait_ge(state_loaded, 16 * (l + 1))
                pool.memset(ext[:, :, 0:3], 0.0).then_inc(ext_history, 1)
                pool.tensor_copy(seqs(ext)[:, :, :, 0:3], stin[:, 0:240].rearrange("p (k b j) -> p k b j", k=KR, b=SB))\
                    .then_inc(ext_history, 1)
                pool.wait_ge(z_evac, z0 + 1)
                pool.wait_ge(kcache_loaded, 16 * (l + 1))
                pool.tensor_copy(kc[:, :, WIN:WIN + SS], qkx[:, 8, TP:T].rearrange("p (b s) -> p b s", b=SB))\
                    .then_inc(k_ready, 1)
                if l == 1:
                    pool.wait_ge(state_out_done, 16)
                pool.wait_ge(ext_ready, 2 * (l + 1))
                pool.tensor_copy(stout[:, 0:30].rearrange("p (k j) -> p k j", k=KR), ext[:, :, TP:TP + 3])\
                    .then_inc(conv_saved, 1)
                pool.tensor_copy(stout[:, 30:270].rearrange("p (k b j) -> p k b j", k=KR, b=SB), seqs(ext)[:, :, :, SS:EP])\
                    .then_inc(conv_saved, 1)
                pool.wait_ge(k_ready, l + 1)
                pool.wait_ge(z_evac, z0 + 2)
                pool.dma_start(o_kp[l], qkx[:, 8, TP - WIN:TP]).then_inc(kv_out_done, 16)
                pool.dma_start(o_vp[l], qkx[:, 9, TP - WIN:TP]).then_inc(kv_out_done, 16)
                pool.dma_start(o_ks[l], kc[:, :, SS:WIN + SS]).then_inc(kv_out_done, 16)
                pool.wait_ge(vcache_loaded, 16 * (l + 1))
                pool.dma_start(o_vs[l, 0:WIN - SS], vc[SS:WIN, :, :]).then_inc(kv_out_done, 16)
                pool.wait_ge(v_ready, 4 * (l + 1))
                pool.dma_start(o_vs[l, WIN - SS:WIN], vnew[:, :, :]).then_inc(kv_out_done, 16)
                pool.wait_ge(rec_ready, KR * (l + 1))
                pool.tensor_copy(stout[:, 270:280].rearrange("p (k j) -> p k j", k=KR), hs[:, :, TP - 1:TP])\
                    .then_inc(h_saved, 1)
                pool.tensor_copy(stout[:, 280:360].rearrange("p (k b) -> p k b", k=KR),
                                 seqs(hs)[:, :, :, EP - 1]).then_inc(h_saved, 1)
                pool.wait_ge(h_saved, 2 * (l + 1))
                pool.wait_ge(conv_saved, 2 * (l + 1))
                pool.dma_start(o_state[l], stout[:, :]).then_inc(state_out_done, 16)
            pool.wait_ge(kv_out_done, 16 * 10)
            pool.wait_ge(state_out_done, 16 * 2)

        @block.scalar
        def _(act):
            def copy(out, in_):
                return nc.scalar.activation(out, in_, ACT.Copy)

            def hi(c, i=0, step=0):
                assert step % RING == 0
                if BASE[1] + N_MIX <= c:
                    return
                act.wait_ge(raw_loaded[c % RING], i * (16 * step // RING) + 16 * (c // RING + 1))
                if c >= SPLIT:
                    act.wait_ge(pe_chunk, i * step + (c - SPLIT + 1))
                copy(whi[c % SPLIT][:, :, :], raw[:, c % RING, :].rearrange("p (k n) -> p k n", n=P)).then_inc(hi_done, 1)

            def norm(n, split=True):
                for k in range(KD):
                    if n == 0:
                        act.wait_ge(x_loaded, 16)
                    elif n < 4:
                        act.wait_ge(x_added, KD * (n - 1) + k + 1)
                    nc.scalar.activation(sq[:, k, :], x[:, k, :], ACT.Square).then_inc(sq_done, 1)
                act.wait_ge(sumsq_done, n + 1)
                nc.scalar.activation(rms[:, :], ps[7][:, 0:T], ACT.Sqrt, bias=eps[:, :], scale=1.0 / D).then_inc(rms_done, 1)
                if split:
                    for k in range(KD):
                        act.wait_ge(nt_done, KD * n + k + 1)
                        copy(xnh[:, k, :], nt[:, k, :]).then_inc(xhi_done, 1)

            act.wait_ge(c_ready, 1)
            nc.scalar.activation(sp_e[:, :], sp_e[:, :], ACT.Exp, scale=-1.0).then_inc(sp_exp, 1)
            act.wait_ge(c_ready, 2)

            hi(0)
            hi(1)
            for l in range(2):
                c0, u0 = BASE[l], NU * l
                norm(2 * l)

                def project(m0, n, tile0):
                    with act.Fori(0, n // 4) as i:
                        for j in range(4):
                            c = c0 + m0 + j
                            hi(c + 2, i, 4)
                            act.wait_ge(pe_chunk, i * 4 + (c + 1))
                            copy(qkx[:, bass.ds(i * 4 + (tile0 + j), 1), :], ps[c % 2][:, 0:T]).then_inc(z_evac, 1)

                project(0, 12, 8)
                project(12, 8, 0)

                act.wait_ge(vt_mm, l + 1)
                copy(vp[:, 0:2, :], ps[6][:, 0:256].rearrange("p (t n) -> p t n", t=2)).then_inc(v_ready, 1)
                copy(vp[0:TP - 256, 2, :], ps[6][0:TP - 256, 256:384]).then_inc(v_ready, 1)
                copy(vnew[:, 0:4, :], ps[5][0:SS, :].rearrange("p (b n) -> p b n", b=4)).then_inc(v_ready, 1)
                copy(vnew[:, 4:8, :], ps[7][0:SS, :].rearrange("p (b n) -> p b n", b=4)).then_inc(v_ready, 1)

                def exps(u):
                    kind, _ = ATT_UNITS[u]
                    n, w, q = ATT_N[kind], ATT_W[kind], u % 2
                    act.wait_ge(s_neg, u0 + u + 1)
                    for i in range(n):
                        nc.scalar.activation(sp[q][:, i * w:(i + 1) * w], sp[q][:, i * w:(i + 1) * w], ACT.Exp,
                                             bias=neg[q][:, i:i + 1], accum_out=rsum[q][:, i:i + 1])
                    nc.scalar.activation(esk[q][:, 0:n], dsk[q][:, 0:n], ACT.Exp).then_inc(p_exp, 1)

                def pt_copy(u):
                    act.wait_ge(pt_mm, u0 + u + 1)
                    src = ps[6][:, :].rearrange("p (i n) -> p i n", i=4)
                    kind, _ = ATT_UNITS[u]
                    if kind in "AB":
                        copy(pt[u % 2][:, :, :], src).then_inc(pt_copied, 2)
                    else:
                        few = ATT_W[kind] - P
                        copy(pt[u % 2][:, 0:2, :], src[:, 0:2, :]).then_inc(pt_copied, 1)
                        copy(pt[u % 2][0:few, 2:4, :], src[0:few, 2:4, :]).then_inc(pt_copied, 1)

                def out(u):
                    act.wait_ge(pv_mm, u0 + u + 1)
                    dst, src = att_part(u)
                    copy(dst, src).then_inc(o_evac, 1)

                exps(0)
                for s in range(NU + 2):
                    c = c0 + N_Q + s - 1
                    if 1 <= s <= N_MG:
                        hi(c + 2)
                    if 1 <= s <= NU:
                        pt_copy(s - 1)
                    if s >= 2:
                        out(s - 2)
                    if 1 <= s <= N_MG:
                        act.wait_ge(pe_chunk, c + 1)
                        copy(gates[:, s - 1, :], ps[c % 2][:, 0:T]).then_inc(z_evac, 1)
                    if s + 1 < NU:
                        exps(s + 1)

                act.wait_ge(z_evac, N_IN * l + N_Q + N_MG)
                for j in range(N_G):
                    c = c0 + C_G + j
                    hi(c + 2)
                    nc.scalar.activation(gates[:, 2 * j:2 * j + 2, :], gates[:, 2 * j:2 * j + 2, :], ACT.Sigmoid).then_inc(gates_ready, 1)
                    act.wait_ge(pe_chunk, c + 1)
                    if j == 2:
                        act.wait_ge(kv_out_done, 16 * 5 * (l + 1))
                    half, gate, part = j // 4, j // 2 % 2, j % 2
                    dst, bias = (ig, "b_i") if gate else (rg, "b_a")
                    for i in ((3, 4) if part else (0, 1, 2)):
                        t = 5 * half + i
                        nc.scalar.activation(dst[:, t, :], ps[2 + i][:, 0:C], ACT.Sigmoid,
                                             bias=p_(l, bias)[:, t:t + 1]).then_inc(gate_evac, 1)

                act.wait_ge(gate_evac, 20 * (l + 1))
                for t in range(KR):
                    c, k = c0 + C_Y + t, KR * l + t
                    hi(c + 2)
                    nc.scalar.activation(asq[:, t, :], rg[:, t, :], ACT.Exp, scale=c2[:, k:k + 1])
                    nc.scalar.activation(mul[:, t, :], rg[:, t, :], ACT.Tanh, scale=cm[:, k:k + 1])
                    ins = nc.scalar.activation(rg[:, t, :], rg[:, t, :], ACT.Exp, scale=c1[:, k:k + 1])
                    if t % 2:
                        ins.then_inc(lru_pair, 1)
                    act.wait_ge(pe_chunk, c + 1)
                    if t == KR - 1:
                        for k in range(KD):
                            copy(atth[:, k, :], qkx[:, k, :]).then_inc(att_hi, 1)
                    copy(yr[:, t, :], ps[t % 2][:, 0:T]).then_inc(z_evac, 1)
                act.wait_ge(m2_done, 5 * (l + 1))
                nc.scalar.activation(mul[:, :, :], mul[:, :, :], ACT.Sqrt).then_inc(m_sqrt, 1)

                def rec_high(t):
                    act.wait_ge(rec_ready, KR * l + t + 1)
                    copy(rech[:, t, :], rect[:, t, :]).then_inc(rec_hi, 1)

                act.wait_ge(z_evac, N_IN * (l + 1))
                for j in range(N_A):
                    hi(c0 + C_A + j + 2)
                    if j == 0:
                        nc.scalar.activation(yr[:, :, :], yr[:, :, :], ACT.Gelu_apprx_tanh).then_inc(yr_ready, 1)
                    if 2 <= j <= 6:
                        rec_high(2 * (j - 2))
                        rec_high(2 * (j - 2) + 1)
                for j in range(N_R + N_O):
                    hi(c0 + C_R + j + 2)
                norm(2 * l + 1, split=(l == 0))

                if l == 0:
                    f0 = N_MIX

                    def gate_silu(m, i=0):
                        q = m % 2
                        act.wait_ge(pe_chunk, i * 4 + (f0 + 2 * m + 1))
                        if m >= 2:
                            act.wait_ge(ffn_h, i * 2 + (m - 1))
                        nc.scalar.activation(sg[q][:, :], ps[2 * q][:, 0:T], ACT.Silu).then_inc(ffn_silu, 1)

                    for j in range(4):
                        hi(f0 + j + 2)
                        if j % 2 == 0:
                            gate_silu(j // 2)
                    with act.Fori(0, KF // 2 - 1) as i:
                        for j in range(4):
                            hi(f0 + 4 + j + 2, i, 4)
                            if j % 2 == 0:
                                gate_silu(2 + j // 2, i)
                    with act.Fori(0, KF // 4) as i:
                        for j in range(4):
                            hi(f0 + 2 * KF + j + 2, i, 4)

            for t in range(3):
                for f in range(2):
                    n = 2 * t + f
                    rows = TT[t][1]
                    act.wait_ge(tok_mm, n + 1)
                    copy(tokh[0:rows, t, 512 * f:512 * f + 512], ps[n][0:rows, :]).then_inc(tok_hi, 1)
            act.wait_ge(top_gap, 1)
            nc.scalar.activation(e2[:, :], dlt[:, :], ACT.Exp).then_inc(top_exp, 1)
            act.wait_ge(rounds_ready, 1)
            n_it = act.value_load(nit[0:1, 0:1], min_val=8, max_val=24)

            def mhi(q, i=0):
                act.wait_ge(mraw_loaded[q % MRING], i * (16 * N_EXP // MRING) + 16 * (q // MRING + 1))
                if q >= MSPLIT or not isinstance(i, int):
                    act.wait_ge(mpe_chunk, i * N_EXP + (q - MSPLIT + 1))
                copy(mwhi[q % MSPLIT][:, :, :], mraw[:, q % MRING, :].rearrange("p (k n) -> p k n", n=512)).then_inc(mhi_done, 1)

            def gather_evac(f, e):
                act.wait_ge(g_mm, e * 4 + (f + 1))
                dst = (xeh, xel)[f // 2][:, 4 * (f % 2):4 * (f % 2) + 4, :]
                copy(dst, ps[5 + f % 2][:, :].rearrange("p (k n) -> p k n", k=4)).then_inc(g_evac, 1)

            def selt_evac(e):
                act.wait_ge(st_mm, e + 1)
                copy(selt[:, :], ps[7][:, 0:T]).then_inc(st_evac, 1)
                copy(cws[:, :], ps[7][:, 340:341]).then_inc(st_evac, 1)

            for f in range(4):
                gather_evac(f, 0)
            selt_evac(0)
            for q in range(LEAD):
                mhi(q)
            nc.scalar.activation(e2[:, :], dlt[:, :], ACT.Silu)
            with act.Fori(0, n_it) as i:
                for j in range(N_EXP):
                    act.wait_ge(mraw_loaded[(j + LEAD) % MRING], i * (16 * N_EXP // MRING) + 16 * ((j + LEAD) // MRING + 1))
                    if j:
                        act.wait_ge(mpe_chunk, i * N_EXP + j)
                    copy(mwhi[(j + LEAD) % MSPLIT][:, :, :],
                         mraw[:, (j + LEAD) % MRING, :].rearrange("p (k n) -> p k n", n=512)).then_inc(mhi_done, 1)
                    if j in (3, 11, 23):
                        n = (3, 11, 23).index(j)
                        act.wait_ge(mpe_chunk, i * N_EXP + (j + 1))
                        if n:
                            act.wait_ge(m_h, i * 3 + n)
                        nc.scalar.activation(esg[:, :], ps[0][:, :], ACT.Silu).then_inc(m_silu, 1)
                    if j in (12, 24, 31):
                        n = (12, 24, 31).index(j)
                        act.wait_ge(t_mm, i * 3 + (n + 1))
                        copy(hth[:, :, :], ps[4][:, :].rearrange("p (k n) -> p k n", k=4)).then_inc(ht_hi, 1)
                    if j == 31:
                        gather_evac(0, i + 1)
                        gather_evac(1, i + 1)
                act.wait_ge(mpe_chunk, i * N_EXP + N_EXP)
                act.wait_ge(st_evac, i * 2 + 2)
                for h in range(2):
                    nc.scalar.activation(yeh[:, 512 * h:512 * h + 512], ps[2 + h][:, :], ACT.Copy,
                                         scale=cws[:, 0:1]).then_inc(ye_hi, 1)
                gather_evac(2, i + 1)
                gather_evac(3, i + 1)
                act.wait_ge(ye_lo, i * 2 + 2)
                selt_evac(i + 1)
            act.wait_ge(m_add, n_it * KD)
            norm(4, split=False)


        @block.vector
        def _(ve):
            v = nc.vector
            steps = [0]

            def step(ins):
                steps[0] += 1
                ins.then_inc(dve_step, 1)
                ve.wait_ge(dve_step, steps[0])

            def f32(t):
                return t.bitcast(F32)

            def lo(c, i=0, step_=0):
                assert step_ % RING == 0
                if BASE[1] + N_MIX <= c:
                    return
                ve.wait_ge(hi_done, i * step_ + (c + 1))
                v.tensor_tensor(wlo[c % SPLIT][:, :, :], raw[:, c % RING, :].rearrange("p (k n) -> p k n", n=P),
                                f32(whi[c % SPLIT][:, :, :]), ALU.subtract).then_inc(lo_done, 1)

            def norm(n, split=True):
                g = gain(n)
                ve.wait_ge(rms_done, n + 1)
                step(v.reciprocal(rstd[:, :], rms[:, :]))

                def low(k):
                    ve.wait_ge(xhi_done, KD * n + k + 1)
                    v.tensor_tensor(xnl[:, k, :], nt[:, k, :], f32(xnh[:, k, :]), ALU.subtract).then_inc(xlo_done, 1)

                for k in range(KD):
                    v.scalar_tensor_tensor(out=nt[:, k, :], in0=x[:, k, :], scalar=g[:, k:k + 1], in1=rstd[:, :],
                                           op0=ALU.mult, op1=ALU.mult).then_inc(nt_done, 1)
                    if split and k >= 1:
                        low(k - 1)
                if split:
                    low(KD - 1)

            step(v.memset(eps[:, :], EPS))
            ve.wait_ge(consts_loaded, 48)
            a, b = PAR["lam"]
            lam = par[:, :, a:b]
            two = lambda t: t[:, :].rearrange("p (l k) -> p l k", l=2)
            v.scalar_tensor_tensor(out=two(sp_e), in0=lam, scalar=-1.0, in1=lam, op0=ALU.mult, op1=ALU.max).then_inc(c_ready, 1)
            step(v.tensor_scalar(two(sp_q), lam, -1.0, 0.0, ALU.mult, ALU.max))
            a, b = PAR["sinks"]
            step(v.tensor_scalar(nsink[:, :].rearrange("p (l k) -> p l k", l=2), par[:, :, a:b], -1.0, None, ALU.mult))
            ve.wait_ge(sp_exp, 1)
            step(v.tensor_scalar(sp_p[:, :], sp_e[:, :], 2.0, None, ALU.add))
            step(v.reciprocal(sp_z[:, :], sp_p[:, :]))
            step(v.tensor_tensor(sp_z[:, :], sp_z[:, :], sp_e[:, :], ALU.mult))
            step(v.tensor_tensor(sp_e[:, :], sp_z[:, :], sp_z[:, :], ALU.mult))
            step(v.tensor_scalar(sp_p[:, :], sp_e[:, :], 1.0 / 15, None, ALU.mult))
            for d in (13, 11, 9, 7, 5, 3):
                step(v.scalar_tensor_tensor(out=sp_p[:, :], in0=sp_p[:, :], scalar=1.0 / d, in1=sp_e[:, :], op0=ALU.add, op1=ALU.mult))
            step(v.scalar_tensor_tensor(out=sp_p[:, :], in0=sp_p[:, :], scalar=1.0, in1=sp_z[:, :], op0=ALU.add, op1=ALU.mult))
            step(v.scalar_tensor_tensor(out=sp_p[:, :], in0=sp_p[:, :], scalar=2.0, in1=sp_q[:, :], op0=ALU.mult, op1=ALU.add))
            v.tensor_scalar(c1[:, :], sp_p[:, :], -8.0, None, ALU.mult)
            v.tensor_scalar(c2[:, :], sp_p[:, :], -16.0, None, ALU.mult)
            v.tensor_scalar(cm[:, :], sp_p[:, :], 8.0, None, ALU.mult).then_inc(c_ready, 1)

            lo(0)
            lo(1)
            for l in range(2):
                c0, u0 = BASE[l], NU * l
                norm(2 * l)
                with ve.Fori(0, 3) as i:
                    for j in range(4):
                        lo(c0 + j + 2, i, 4)

                def lines():
                    ve.wait_ge(z_evac, N_IN * l + 12)
                    v.tensor_copy(ext[:, :, 3:3 + TP], qkx[:, 10:20, 0:TP]).then_inc(ext_ready, 1)
                    v.tensor_copy(seqs(ext)[:, :, :, 3:EP],
                                  qkx[:, 10:20, TP:T].rearrange("p k (b s) -> p k b s", b=SB)).then_inc(ext_ready, 1)
                    ve.wait_ge(ext_ready, 2 * (l + 1))
                    ve.wait_ge(ext_history, 2 * (l + 1))

                def conv(t):
                    w = p_(l, "w_conv")
                    step(v.tensor_scalar(xc[:, t, :], ext[:, t, 0:C], w[:, t:t + 1], p_(l, "b_conv")[:, t:t + 1], ALU.mult, ALU.add))
                    for j in range(1, CW):
                        step(v.scalar_tensor_tensor(out=xc[:, t, :], in0=ext[:, t, j:j + C], scalar=w[:, KR * j + t:KR * j + t + 1],
                                                    in1=xc[:, t, :], op0=ALU.mult, op1=ALU.add))
                    step(v.tensor_copy(xch[:, t, :], xc[:, t, :]))
                    if t == 0:
                        ve.wait_ge(conv_saved, 2 * (l + 1))
                    v.tensor_tensor(xcl[:, t, :], xc[:, t, :], f32(xch[:, t, :]), ALU.subtract).then_inc(xc_split, 1)

                lo(c0 + 14)
                lines()
                for j in range(13, N_Q):
                    lo(c0 + j + 2)
                    if j % 2 == 0:
                        conv(j // 2 - 7)

                def maxima(u):
                    kind, k = ATT_UNITS[u]
                    n, w, q = ATT_N[kind], ATT_W[kind], u % 2
                    mask = const("m" + kind)
                    s0 = SINK0[kind] + (n * k if kind in "AB" else 0)
                    ns = nsink[:, 36 * l + s0:36 * l + s0 + n]
                    ve.wait_ge(s_mm, u0 + u + 1)
                    if u >= 2:
                        ve.wait_ge(pt_mm, u0 + u - 1)
                    if kind == "D":
                        for g in range(2):
                            r = slice(64 * g, 64 * g + 64)
                            ins = v.scalar_tensor_tensor(
                                out=sp[q][r, 0:n * w].rearrange("p (i w) -> p i w", i=n),
                                in0=ps[2 + 2 * q + g][r, 0:n * w].rearrange("p (i w) -> p i w", i=n), scalar=HD ** -0.5,
                                in1=mask[r, :].unsqueeze(1).to_broadcast([64, n, w]), op0=ALU.mult, op1=ALU.add)
                    else:
                        per = n * w // 2
                        for g in range(2):
                            ins = v.scalar_tensor_tensor(
                                out=sp[q][:, g * per:(g + 1) * per], in0=ps[2 + 2 * q + g][:, 0:per], scalar=HD ** -0.5,
                                in1=mask[:, 0:per], op0=ALU.mult, op1=ALU.add)
                    step(ins)
                    step(v.tensor_reduce(mx[q][:, 0:n], sp[q][:, 0:n * w].rearrange("p (i w) -> p i w", i=n), AX, ALU.max))
                    step(v.scalar_tensor_tensor(out=neg[q][:, 0:n], in0=mx[q][:, 0:n], scalar=-1.0, in1=ns, op0=ALU.mult, op1=ALU.min))
                    v.tensor_tensor(dsk[q][:, 0:n], neg[q][:, 0:n], ns, ALU.subtract).then_inc(s_neg, 1)

                def weights(u):
                    kind, _ = ATT_UNITS[u]
                    n, w, q = ATT_N[kind], ATT_W[kind], u % 2
                    ve.wait_ge(p_exp, u0 + u + 1)
                    step(v.tensor_tensor(rinv[q][:, 0:n], rsum[q][:, 0:n], esk[q][:, 0:n], ALU.add))
                    step(v.reciprocal(rinv[q][:, 0:n], rinv[q][:, 0:n]))
                    for i in range(n):
                        ins = v.tensor_scalar(sp[q][:, i * w:(i + 1) * w], sp[q][:, i * w:(i + 1) * w], rinv[q][:, i:i + 1], None, ALU.mult)
                    ins.then_inc(p_norm, 1)

                maxima(0)
                ve.wait_ge(z_evac, N_IN * l + N_Q)
                v.tensor_copy(qt[:, 0:128].rearrange("p (h s) -> p h s", h=KD), qkx[:, 0:8, 256:TP])
                v.tensor_copy(qt[:, 128:].rearrange("p (b h s) -> p h b s", b=SB, h=KD),
                              qkx[:, 0:8, TP:T].rearrange("p h (b s) -> p h b s", b=SB)).then_inc(qt_ready, 1)
                weights(0)
                for s in range(NU):
                    if s + 1 < NU:
                        maxima(s + 1)
                    if 1 <= s <= N_MG:
                        lo(c0 + N_Q + s + 1)
                    if s % 2 == 0 and s < 14:
                        conv(3 + s // 2)
                    if s + 1 < NU:
                        weights(s + 1)
                for j in range(N_G):
                    lo(c0 + C_G + j + 2)
                ve.wait_ge(gate_evac, 20 * (l + 1))
                step(v.tensor_tensor(ig[:, :, :], ig[:, :, :], xc[:, :, :], ALU.mult))
                for t in range(KR):
                    lo(c0 + C_Y + t + 2)
                    if t % 2:
                        ve.wait_ge(lru_pair, 5 * l + t // 2 + 1)
                        pair = slice(t - 1, t + 1)
                        v.scalar_tensor_tensor(out=mul[:, pair, :], in0=asq[:, pair, :], scalar=1.0, in1=mul[:, pair, :],
                                               op0=ALU.add, op1=ALU.mult).then_inc(m2_done, 1)
                for k in range(KD):
                    ve.wait_ge(att_hi, KD * l + k + 1)
                    v.tensor_tensor(attl[:, k, :], qkx[:, k, :], f32(atth[:, k, :]), ALU.subtract).then_inc(att_lo, 1)
                v.memset(seqs(rg)[:, :, :, 2], 0.0)

                def scan(t):
                    step(v.tensor_tensor_scan(hs[:, t, :], rg[:, t, :], ig[:, t, :], 0.0, ALU.mult, ALU.add))
                    v.tensor_tensor(rect[:, t, 0:TP], hs[:, t, 0:TP], yr[:, t, 0:TP], ALU.mult)
                    v.tensor_tensor(rect[:, t, TP:T].rearrange("p (b s) -> p b s", b=SB), seqs(hs)[:, t, :, 3:EP],
                                    yr[:, t, TP:T].rearrange("p (b s) -> p b s", b=SB), ALU.mult).then_inc(rec_ready, 1)

                def rec_low(t):
                    ve.wait_ge(rec_hi, KR * l + t + 1)
                    v.tensor_tensor(recl[:, t, :], rect[:, t, :], f32(rech[:, t, :]), ALU.subtract).then_inc(rec_split, 1)

                for j in range(N_A):
                    c = c0 + C_A + j
                    lo(c + 2)
                    ve.wait_ge(pe_chunk, c + 1)
                    if j == 0:
                        ve.wait_ge(gates_ready, KD * (l + 1))
                    v.tensor_tensor(gates[:, j, :], ps[j % 2][:, 0:T], gates[:, j, :], ALU.mult).then_inc(ap_post, 1)
                    if j == 0:
                        ve.wait_ge(m_sqrt, l + 1)
                        step(v.memset(mul[:, :, 0:1], 1.0))
                        step(v.tensor_tensor(ig[:, :, :], ig[:, :, :], mul[:, :, :], ALU.mult))
                        ve.wait_ge(state_loaded, 16 * (l + 1))
                        step(v.tensor_copy(seqs(ig)[:, :, :, 2], stin[:, 240:320].rearrange("p (k b) -> p k b", k=KR)))
                        ve.wait_ge(yr_ready, l + 1)
                    if 1 <= j <= 5:
                        scan(2 * (j - 1))
                        scan(2 * (j - 1) + 1)
                    if 2 <= j <= 6:
                        rec_low(2 * (j - 2))
                        rec_low(2 * (j - 2) + 1)

                ve.wait_ge(h_saved, 2 * (l + 1))
                m = 0
                for j in range(N_R):
                    c = c0 + C_R + j
                    lo(c + 2)
                    while m < KD and (KR * m + KR - 1) // 8 == j:
                        ve.wait_ge(pe_chunk, c + 1)
                        ins = v.tensor_tensor(gates[:, KD + m, :], ps[m % 2][:, 0:T], gates[:, KD + m, :], ALU.mult)
                        ins.then_inc(rp_post, 1)
                        ve.wait_ge(rp_post, KD * l + m + 1)
                        step(v.tensor_tensor(gates[:, m, :], gates[:, m, :], gates[:, KD + m, :], ALU.add))
                        step(v.tensor_copy(mgh[:, m, :], gates[:, m, :]))
                        v.tensor_tensor(mgl[:, m, :], gates[:, m, :], f32(mgh[:, m, :]), ALU.subtract).then_inc(mg_split, 1)
                        m += 1

                for m in range(KD):
                    c = c0 + C_O + m
                    lo(c + 2)
                    ve.wait_ge(pe_chunk, c + 1)
                    v.tensor_tensor(x[:, m, :], ps[m % 2][:, 0:T], x[:, m, :], ALU.add).then_inc(x_added, 1)
                norm(2 * l + 1, split=(l == 0))

                if l == 0:
                    f0 = N_MIX

                    def hidden(m, i=0):
                        q = m % 2
                        ve.wait_ge(pe_chunk, i * 4 + (f0 + 2 * m + 2))
                        ve.wait_ge(ffn_silu, i * 2 + (m + 1))
                        v.tensor_tensor(hh[:, :], ps[2 * q + 1][:, 0:T], sg[q][:, :], ALU.mult).then_inc(ffn_h, 1)
                        ve.wait_ge(ffn_h, i * 2 + (m + 1))
                        v.tensor_copy(hfh[:, bass.ds(i * 2 + m, 1), :], hh[:, :].unsqueeze(1)).then_inc(ffn_hi, 1)
                        ve.wait_ge(ffn_hi, i * 2 + (m + 1))
                        v.tensor_tensor(hfl[:, bass.ds(i * 2 + m, 1), :], hh[:, :].unsqueeze(1),
                                        f32(hfh[:, bass.ds(i * 2 + m, 1), :]), ALU.subtract).then_inc(ffn_lo, 1)
                        ve.wait_ge(ffn_lo, i * 2 + (m + 1))

                    with ve.Fori(0, KF // 2) as i:
                        for j in range(4):
                            lo(f0 + j + 2, i, 4)
                            if j % 2:
                                hidden(j // 2, i)
                    with ve.Fori(0, 2) as i:
                        for j in range(12):
                            c = f0 + 2 * KF + j
                            lo(c + 2, i, 12)
                            if j % 3 == 2:
                                m = j // 3
                                ve.wait_ge(pe_chunk, i * 12 + (c + 1))
                                xm = x[:, bass.ds(i * 4 + m, 1), :]
                                v.tensor_tensor(xm, ps[4 + m % 2][:, 0:T].unsqueeze(1), xm, ALU.add).then_inc(x_added, 1)

            for t in range(3):
                for f in range(2):
                    n = 2 * t + f
                    rows = TT[t][1]
                    ve.wait_ge(tok_hi, n + 1)
                    v.tensor_tensor(tokl[0:rows, t, 512 * f:512 * f + 512], ps[n][0:rows, :],
                                    f32(tokh[0:rows, t, 512 * f:512 * f + 512]), ALU.subtract).then_inc(tok_lo, 1)

            def e3(t):
                return t[:, :].rearrange("p (t e) -> p t e", e=NE)

            def per_row(t):
                return t[:, :].unsqueeze(2).to_broadcast([P, 3, NE])

            step(v.memset(lg[:, :], 0.0))
            ve.wait_ge(router_mm, 1)
            rows = TT[2][1]
            v.tensor_tensor(lg[:, 0:16], ps[6][:, 0:16], brt[:, 0:16], ALU.add)
            step(v.tensor_tensor(lg[0:rows, 16:24], ps[6][0:rows, 16:24], brt[0:rows, 16:24], ALU.add))
            rank = const("rank")

            def largest(lgt, top, oh):
                step(v.tensor_reduce(top[:, :], e3(lgt), AX, ALU.max))
                step(v.tensor_tensor(e3(eq), e3(lgt), per_row(top), ALU.is_equal))
                step(v.tensor_tensor(eq[:, :], eq[:, :], rank, ALU.mult))
                step(v.tensor_reduce(rk[:, :], e3(eq), AX, ALU.max))
                step(v.tensor_tensor(e3(oh), rank.rearrange("p (t e) -> p t e", e=NE), per_row(rk), ALU.is_equal))

            largest(lg, top1, oh1)
            step(v.scalar_tensor_tensor(out=lg2[:, :], in0=oh1[:, :], scalar=-3.0e38, in1=lg[:, :], op0=ALU.mult, op1=ALU.add))
            largest(lg2, top2, oh2)
            v.tensor_tensor(dlt[:, :], top2[:, :], top1[:, :], ALU.subtract).then_inc(top_gap, 1)
            step(v.tensor_tensor(msk[:, :], oh1[:, :], oh2[:, :], ALU.add))
            v.tensor_tensor(msk[:, :], msk[:, :], const("valid"), ALU.mult).then_inc(mask_ready, 1)
            ve.wait_ge(top_exp, 1)
            step(v.tensor_scalar(w1[:, :], e2[:, :], 1.0, None, ALU.add))
            step(v.reciprocal(w1[:, :], w1[:, :]))
            step(v.tensor_tensor(w2[:, :], e2[:, :], w1[:, :], ALU.mult))
            step(v.tensor_tensor(e3(oh1), e3(oh1), per_row(w1), ALU.mult))
            step(v.tensor_tensor(e3(oh2), e3(oh2), per_row(w2), ALU.mult))
            step(v.tensor_tensor(cwt[:, :], oh1[:, :], oh2[:, :], ALU.add))
            ve.wait_ge(pos_mm, 1)
            step(v.scalar_tensor_tensor(out=pm[:, :], in0=ps[7][:, 0:24], scalar=1.0, in1=msk[:, :], op0=ALU.add, op1=ALU.mult))
            step(v.memset(pmx[:, :], -1.0))
            step(v.memset(cwx[:, :], 0.0))
            for r in range(3):
                dst = pmx[:, :].rearrange("p (t s) -> p t s", t=3)[:, :, NE * r:NE * r + NE]
                v.tensor_scalar(dst, e3(pm), 1.0, float(SLOTS * r), ALU.subtract, ALU.subtract)
                dst = cwx[:, :].rearrange("p (t s) -> p t s", t=3)[:, :, NE * r:NE * r + NE]
                step(v.tensor_copy(dst, e3(cwt)))
            step(v.tensor_reduce(cnt[:, :], ps[7][:, 24:32], AX, ALU.max))
            step(v.tensor_scalar(c_a[:, :], cnt[:, :], float(SLOTS), None, ALU.is_gt))
            step(v.tensor_scalar(cnt[:, :], cnt[:, :], float(2 * SLOTS), None, ALU.is_gt))
            step(v.tensor_tensor(cnt[:, :], cnt[:, :], c_a[:, :], ALU.add))
            v.tensor_scalar(nit[:, :], cnt[:, :], float(NE), float(NE), ALU.mult, ALU.add).then_inc(rounds_ready, 1)
            ve.wait_ge(rounds_ready, 1)
            n_it = ve.value_load(nit[0:1, 0:1], min_val=8, max_val=24)

            def select(e):
                v.tensor_copy(cur[:, 0:3], pmx[:, :].rearrange("p (t s) -> p t s", t=3)[:, :, bass.ds(e, 1)].rearrange("p t s -> p (t s)"))
                v.tensor_copy(cur[:, 3:6], cwx[:, :].rearrange("p (t s) -> p t s", t=3)[:, :, bass.ds(e, 1)].rearrange("p t s -> p (t s)")).then_inc(cur_ready, 1)
                ve.wait_ge(cur_ready, e + 1)
                for t in range(3):
                    ins = v.tensor_scalar(sel[:, t, :], const("iota"), cur[:, t:t + 1], None, ALU.is_equal)
                ins.then_inc(sel_built, 1)

            def mlo(q, i=0):
                ve.wait_ge(mhi_done, i * N_EXP + (q + 1))
                v.tensor_tensor(mwlo[q % MSPLIT][:, :, :], mraw[:, q % MRING, :].rearrange("p (k n) -> p k n", n=512),
                                f32(mwhi[q % MSPLIT][:, :, :]), ALU.subtract).then_inc(mlo_done, 1)

            select(0)
            for q in range(LEAD):
                mlo(q)
            with ve.Fori(0, n_it) as i:
                for j in range(N_EXP):
                    mlo(j + LEAD, i)
                    if j == 4:
                        ve.wait_ge(st_mm, i + 1)
                        select(i + 1)
                    if j in (7, 15, 27):
                        n = (7, 15, 27).index(j)
                        ve.wait_ge(mpe_chunk, i * N_EXP + (j + 1))
                        ve.wait_ge(m_silu, i * 3 + (n + 1))
                        if n:
                            ve.wait_ge(t_mm, i * 3 + n)
                        v.tensor_tensor(eh[:, :], ps[1][:, :], esg[:, :], ALU.mult).then_inc(m_h, 1)
                    if j in (12, 24, 31):
                        n = (12, 24, 31).index(j)
                        ve.wait_ge(ht_hi, i * 3 + (n + 1))
                        v.tensor_tensor(htl[:, :, :], ps[4][:, :].rearrange("p (k n) -> p k n", k=4),
                                        f32(hth[:, :, :]), ALU.subtract).then_inc(ht_lo, 1)
                for h in range(2):
                    ve.wait_ge(ye_hi, i * 2 + (h + 1))
                    v.scalar_tensor_tensor(out=yel[:, 512 * h:512 * h + 512], in0=ps[2 + h][:, :], scalar=cws[:, 0:1],
                                           in1=f32(yeh[:, 512 * h:512 * h + 512]), op0=ALU.mult, op1=ALU.subtract).then_inc(ye_lo, 1)
                for m in range(KD):
                    ve.wait_ge(sc_mm, i * KD + (m + 1))
                    v.tensor_tensor(x[:, m, :], ps[(7, 4)[m % 2]][:, 0:T], x[:, m, :], ALU.add).then_inc(m_add, 1)
            norm(4, split=False)

        @block.tensor
        def _(pe):
            mm = nc.tensor.matmul

            def three(out, wh, wl, xh, xl, start, stop):
                mm(out, wh, xh, start=start, stop=False)
                mm(out, wh, xl, start=False, stop=False)
                return mm(out, wl, xh, start=False, stop=stop)

            def chunk(c, out, xh, xl, i=0, step_=0, start=True, stop=True, ready=None, count=0):
                pe.wait_ge(lo_done, i * step_ + (c + 1))
                for k in range(8):
                    if ready is not None:
                        pe.wait_ge(ready, count + k + 1)
                    ins = three(out, whi[c % SPLIT][:, k, :], wlo[c % SPLIT][:, k, :], xh[:, k, :], xl[:, k, :],
                                start and k == 0, stop and k == 7)
                ins.then_inc(pe_chunk, 1)

            def norm(n):
                for k in range(KD):
                    pe.wait_ge(sq_done, KD * n + k + 1)
                    ins = mm(ps[7][:, 0:T], ones, sq[:, k, :], start=k == 0, stop=k == KD - 1)
                ins.then_inc(sumsq_done, 1)

            pe.wait_ge(consts_loaded, 48)
            for l in range(2):
                c0, u0 = BASE[l], NU * l
                norm(2 * l)
                chunk(c0, ps[0][:, 0:T], xnh, xnl, ready=xlo_done, count=16 * l)
                chunk(c0 + 1, ps[1][:, 0:T], xnh, xnl)
                with pe.Fori(0, (N_Q - 2) // 2) as i:
                    for j in range(2):
                        pe.wait_ge(z_evac, i * 2 + (N_IN * l + j + 1))
                        chunk(c0 + 2 + j, ps[j % 2][:, 0:T], xnh, xnl, i, 2)

                pe.wait_ge(z_evac, N_IN * l + 2)
                vt = qkx[:, 9, :]
                for t in range(3):
                    a, b = 128 * t, min(128 * t + 128, TP)
                    nc.tensor.transpose(ps[6][0:b - a, 128 * t:128 * t + 128], vt[:, a:b], ident)
                for b in range(SB):
                    ins = nc.tensor.transpose(ps[(5, 7)[b // 4]][0:SS, 128 * (b % 4):128 * (b % 4) + 128],
                                              vt[:, TP + SS * b:TP + SS * b + SS], ident)
                ins.then_inc(vt_mm, 1)

                def scores(u):
                    kind, k = ATT_UNITS[u]
                    if u >= 2:
                        pe.wait_ge(s_neg, u0 + u - 1)
                    if u == 1:
                        pe.wait_ge(v_ready, 4 * (l + 1))
                    if kind == "A":
                        pe.wait_ge(z_evac, N_IN * l + 12 + 2 * k + 2)
                    elif kind == "C":
                        pe.wait_ge(qt_ready, l + 1)
                    elif kind == "D":
                        pe.wait_ge(k_ready, l + 1)
                    for i in range(2):
                        for g in range(2):
                            r = slice(64 * g, 64 * g + 64)
                            bank = ps[2 + 2 * (u % 2) + g]
                            if kind == "A":
                                ins = mm(bank[:, 128 * i:128 * i + 128], qkx[r, 2 * k + i, 0:128], qkx[r, 8, 0:128], start=True, stop=True)
                            elif kind == "D":
                                b = 2 * k + i
                                w = ATT_W["D"]
                                ins = mm(bank[r, w * i:w * i + w], qt[r, 128 + 64 * b:192 + 64 * b], kc[r, b, :], start=True, stop=True)
                            elif i == 0 and kind == "B":
                                ins = mm(bank[:, 0:256], qkx[r, k, 128:256], qkx[r, 8, 0:256], start=True, stop=True)
                            elif i == 0:
                                ins = mm(bank[:, 0:144], qt[r, 0:128], qkx[r, 8, 128:TP], start=True, stop=True)
                    ins.then_inc(s_mm, 1)

                def turn(u):
                    kind, _ = ATT_UNITS[u]
                    q, w = u % 2, ATT_W[kind]
                    pe.wait_ge(p_norm, u0 + u + 1)
                    if u >= 1:
                        pe.wait_ge(pt_copied, 2 * (u0 + u))
                    for s in range(4):
                        if kind in "AB":
                            out, src = ps[6][:, 128 * s:128 * s + 128], sp[q][:, 128 * s:128 * s + 128]
                        else:
                            n = P if s < 2 else w - P
                            a = w * (s % 2) + (0 if s < 2 else P)
                            out, src = ps[6][0:n, 128 * s:128 * s + 128], sp[q][:, a:a + n]
                        ins = nc.tensor.transpose(out, src, ident)
                    ins.then_inc(pt_mm, 1)

                def values(u):
                    kind, k = ATT_UNITS[u]
                    q = u % 2
                    pe.wait_ge(pt_copied, 2 * (u0 + u + 1))
                    if u >= 1:
                        pe.wait_ge(o_evac, u0 + u)
                    for g in range(2):
                        r = slice(64 * g, 64 * g + 64)
                        if kind == "A":
                            for i in range(2):
                                ins = mm(ps[7][r, 128 * i:128 * i + 128], vp[:, 0, r], pt[q][:, 2 * g + i, :], start=True, stop=True)
                        elif kind == "B":
                            for t in range(2):
                                ins = mm(ps[7][r, 0:128], vp[:, t, r], pt[q][:, 2 * g + t, :], start=t == 0, stop=t == 1)
                        elif kind == "C":
                            few = TP - 256
                            mm(ps[7][r, 0:128], vp[:, 1, r], pt[q][:, g, :], start=True, stop=False)
                            ins = mm(ps[7][r, 0:128], vp[0:few, 2, r], pt[q][0:few, 2 + g, :], start=False, stop=True)
                        else:
                            for i in range(2):
                                b = 2 * k + i
                                out = ps[7][r, 0:128].rearrange("p (h i s) -> p h i s", i=2, s=SS)[:, :, i, :]
                                mm(out, vc[:, b, r], pt[q][:, i, r], start=True, stop=False)
                                ins = mm(out, vnew[:, b, r], pt[q][0:SS, 2 + i, r], start=False, stop=True)
                    ins.then_inc(pv_mm, 1)

                scores(0)
                for s in range(NU + 1):
                    if s + 1 < NU:
                        scores(s + 1)
                    if s < N_MG:
                        pe.wait_ge(z_evac, N_IN * l + N_Q + s - 1)
                        chunk(c0 + N_Q + s, ps[s % 2][:, 0:T], xnh, xnl)
                    if s < NU:
                        turn(s)
                    if s == 1:
                        pe.wait_ge(vcache_loaded, 16 * (l + 1))
                    if s >= 1:
                        values(s - 1)

                for j in range(N_G):
                    c = c0 + C_G + j
                    half, part, pair = j // 4, j % 2, j // 2
                    pe.wait_ge(lo_done, c + 1)
                    slot = 0
                    for i in ((3, 4) if part else (0, 1, 2)):
                        pe.wait_ge(xc_split, KR * l + 5 * half + GATE_IN[i][-1] + 1)
                        if pair:
                            pe.wait_ge(gate_evac, 20 * l + 5 * (pair - 1) + i + 1)
                        for k in GATE_IN[i]:
                            t = 5 * half + k
                            ins = three(ps[2 + i][:, 0:C], whi[c % 2][:, slot, :], wlo[c % 2][:, slot, :], xch[:, t, :],
                                        xcl[:, t, :], k == GATE_IN[i][0], k == GATE_IN[i][-1])
                            slot += 1
                    ins.then_inc(pe_chunk, 1)

                for m in range(KR):
                    pe.wait_ge(z_evac, N_IN * l + N_Q + N_MG + m - 1)
                    chunk(c0 + C_Y + m, ps[m % 2][:, 0:T], xnh, xnl)

                for m in range(N_A):
                    if m < 2:
                        pe.wait_ge(z_evac, N_IN * (l + 1) + m - 1)
                    else:
                        pe.wait_ge(ap_post, KD * l + m - 1)
                    chunk(c0 + C_A + m, ps[m % 2][:, 0:T], atth, attl, ready=None if m else att_lo, count=KD * l)

                pe.wait_ge(ap_post, KD * (l + 1))
                for n in range(KD * KR):
                    m, k, c = n // KR, n % KR, c0 + C_R + n // 8
                    if n % 8 == 0:
                        pe.wait_ge(lo_done, c + 1)
                    if k == 0 and m >= 2:
                        pe.wait_ge(rp_post, KD * l + m - 1)
                    if m == 0:
                        pe.wait_ge(rec_split, KR * l + k + 1)
                    ins = three(ps[m % 2][:, 0:T], whi[c % 2][:, n % 8, :], wlo[c % 2][:, n % 8, :], rech[:, k, :],
                                recl[:, k, :], k == 0, k == KR - 1)
                    if n % 8 == 7:
                        ins.then_inc(pe_chunk, 1)

                for m in range(N_O):
                    if m < 2:
                        pe.wait_ge(rp_post, KD * (l + 1) + m - 1)
                    else:
                        pe.wait_ge(x_added, 16 * l + m - 1)
                    chunk(c0 + C_O + m, ps[m % 2][:, 0:T], mgh, mgl, ready=None if m else mg_split, count=KD * l)
                norm(2 * l + 1)

                if l == 0:
                    f0 = N_MIX
                    def gate_up(m, i=0):
                        q = m % 2
                        if m >= 2:
                            pe.wait_ge(ffn_silu, i * 2 + (m - 1))
                        chunk(f0 + 2 * m, ps[2 * q][:, 0:T], xnh, xnl, i, 4, ready=None if m else xlo_done, count=KD)
                        if m >= 2:
                            pe.wait_ge(ffn_h, i * 2 + (m - 1))
                        chunk(f0 + 2 * m + 1, ps[2 * q + 1][:, 0:T], xnh, xnl, i, 4)

                    gate_up(0)
                    gate_up(1)
                    with pe.Fori(0, KF // 2 - 1) as i:
                        gate_up(2, i)
                        gate_up(3, i)
                    pe.wait_ge(ffn_lo, KF)
                    with pe.Fori(0, 2) as i:
                        for j in range(12):
                            m, third = j // 3, j % 3
                            if third == 0:
                                pe.wait_ge(x_added, i * 4 + (KD + m - 1))
                            chunk(f0 + 2 * KF + j, ps[4 + m % 2][:, 0:T], hfh[:, 8 * third:8 * third + 8, :],
                                  hfl[:, 8 * third:8 * third + 8, :], i, 12, third == 0, third == 2)

            pe.wait_ge(nt_done, 4 * KD)
            for t, (a, rows) in enumerate(TT):
                for f in range(2):
                    for k in range(4):
                        ins = nc.tensor.transpose(ps[2 * t + f][0:rows, 128 * k:128 * k + 128], nt[:, 4 * f + k, a:a + rows], ident)
                    ins.then_inc(tok_mm, 1)
            for t, (a, rows) in enumerate(TT):
                for k in range(KD):
                    ins = mm(ps[6][0:rows, NE * t:NE * t + NE], nt[:, k, a:a + rows], wrt[:, NE * k:NE * k + NE], start=k == 0, stop=k == KD - 1)
            ins.then_inc(router_mm, 1)
            pe.wait_ge(mask_ready, 1)
            for t in range(3):
                for s in range(t + 1):
                    mm(ps[7][:, NE * t:NE * t + NE], const("tri") if s == t else ones, msk[:, NE * s:NE * s + NE], start=s == 0, stop=s == t)
            for s in range(3):
                ins = mm(ps[7][:, 24:32], ones, msk[:, NE * s:NE * s + NE], start=s == 0, stop=s == 2)
            ins.then_inc(pos_mm, 1)
            pe.wait_ge(rounds_ready, 1)
            n_it = pe.value_load(nit[0:1, 0:1], min_val=8, max_val=24)

            def gather(f, e):
                src = (tokh, tokl)[f // 2]
                for k in range(4):
                    for t, (_, rows) in enumerate(TT):
                        col = P * (4 * (f % 2) + k)
                        ins = mm(ps[5 + f % 2][:, 128 * k:128 * k + 128], src[0:rows, t, col:col + P], sel[0:rows, t, :],
                                 start=t == 0, stop=t == 2)
                ins.then_inc(g_mm, 1)

            def selt_and_weights():
                for t, (a, rows) in enumerate(TT):
                    nc.tensor.transpose(ps[7][:, a:a + rows], sel[0:rows, t, :].bitcast(F32), ident[0:rows, 0:rows])
                for t, (a, rows) in enumerate(TT):
                    ins = mm(ps[7][:, 340:341], sel[0:rows, t, :].bitcast(F32), cur[0:rows, 3 + t:4 + t], start=t == 0, stop=t == 2)
                ins.then_inc(st_mm, 1)

            def expert_chunk(j, i, lhs_h, lhs_l, outs, start, stop):
                pe.wait_ge(mlo_done, i * N_EXP + (j + 1))
                s = j % MSPLIT
                for n in range(2):
                    mm(outs[n], lhs_h[n], mwhi[s][:, n, :], start=start[n], stop=False)
                    mm(outs[n], lhs_h[n], mwlo[s][:, n, :], start=False, stop=False)
                    ins = mm(outs[n], lhs_l[n], mwhi[s][:, n, :], start=False, stop=stop[n])
                ins.then_inc(mpe_chunk, 1)

            pe.wait_ge(tok_lo, 6)
            pe.wait_ge(sel_built, 1)
            for f in range(4):
                if f >= 2:
                    pe.wait_ge(g_evac, f - 1)
                gather(f, 0)
            selt_and_weights()
            with pe.Fori(0, n_it) as i:
                def into(j0, bank, ready=None, count=0):
                    if ready is not None:
                        pe.wait_ge(ready, count)
                    for d in range(4):
                        k = 2 * d
                        expert_chunk(j0 + d, i, [xeh[:, k, :], xeh[:, k + 1, :]], [xel[:, k, :], xel[:, k + 1, :]],
                                     [ps[bank][:, :]] * 2, [d == 0, False], [False, d == 3])

                def turn_hidden(n):
                    pe.wait_ge(m_h, i * 3 + (n + 1))
                    if n:
                        pe.wait_ge(ht_lo, i * 3 + n)
                    for k in range(4):
                        ins = nc.tensor.transpose(ps[4][:, 128 * k:128 * k + 128], eh[:, 128 * k:128 * k + 128], ident)
                    ins.then_inc(t_mm, 1)

                def down(j0, n):
                    pe.wait_ge(ht_lo, i * 3 + (n + 1))
                    for d in range(4):
                        expert_chunk(j0 + d, i, [hth[:, d, :]] * 2, [htl[:, d, :]] * 2, [ps[2][:, :], ps[3][:, :]],
                                     [n == 0 and d == 0] * 2, [n == 2 and d == 3] * 2)

                pe.wait_ge(g_evac, i * 4 + 4)
                into(0, 0)
                into(4, 1)
                into(8, 0, m_silu, i * 3 + 1)
                turn_hidden(0)
                into(12, 1, m_h, i * 3 + 1)
                down(16, 0)
                into(20, 0, m_silu, i * 3 + 2)
                turn_hidden(1)
                into(24, 1, m_h, i * 3 + 2)
                down(28, 1)
                turn_hidden(2)
                pe.wait_ge(sel_built, i + 2)
                gather(0, i + 1)
                gather(1, i + 1)
                down(32, 2)
                pe.wait_ge(g_evac, i * 4 + 5)
                gather(2, i + 1)
                pe.wait_ge(g_evac, i * 4 + 6)
                gather(3, i + 1)
                pe.wait_ge(ye_lo, i * 2 + 2)
                for m in range(KD):
                    if m >= 2:
                        pe.wait_ge(m_add, i * KD + (m - 1))
                    out = ps[(7, 4)[m % 2]][:, 0:T]
                    mm(out, yeh[:, P * m:P * m + P], selt[:, :], start=True, stop=False)
                    mm(out, yel[:, P * m:P * m + P], selt[:, :], start=False, stop=True).then_inc(sc_mm, 1)
                pe.wait_ge(m_add, i * KD + KD)
                selt_and_weights()
            norm(4)


def kernel(**inputs):
    import concourse.bacc as bacc
    from concourse.bass_utils import run_bass_kernel_spmd

    f = {k: np.asarray(v) for k, v in inputs.items()}

    def cols(a):
        a = a.reshape(*a.shape[:-1], -1, P)
        return np.moveaxis(a, -1, 0)

    def chunks(w):
        k, m = w.shape
        t = w.reshape(k // P, P, m // P, P).transpose(2, 0, 1, 3).reshape(-1, 8, P, P)
        return t.transpose(0, 2, 1, 3).reshape(-1, P, CH)

    heads = np.arange(1024).reshape(2, 8, HD).transpose(1, 0, 2).reshape(-1)
    o = np.cumsum([0, 1024, 128, 128, REC, REC, D, D])
    order = np.concatenate([np.arange(o[1], o[4]), heads, np.arange(o[5], o[7])])

    def gate_chunks(wa, wi):
        full = []
        for w in (wa, wi):
            z = np.zeros((REC, REC), w.dtype)
            for n in range(16):
                z[80 * n:80 * n + 80, 80 * n:80 * n + 80] = w[n]
            full.append(z)
        out = np.zeros((N_G, P, 8, P), wa.dtype)
        for j in range(N_G):
            half, gate, part = j // 4, j // 2 % 2, j % 2
            slot = 0
            for i in ((3, 4) if part else (0, 1, 2)):
                for k in GATE_IN[i]:
                    a, b = P * (5 * half + k), P * (5 * half + i)
                    out[j, :, slot, :] = full[gate][a:a + P, b:b + P]
                    slot += 1
        return out.reshape(N_G, P, CH)

    w_mix = np.stack([np.concatenate([
        chunks(f["w_in"][l][:, order]), gate_chunks(f["w_rg_a"][l], f["w_rg_i"][l]),
        chunks(f["w_in"][l][:, o[4]:o[5]]), chunks(f["w_att_proj"][l][heads]),
        chunks(f["w_rec_proj"][l]), chunks(f["w_out"][l])]) for l in range(2)])
    gu = np.stack([chunks(f["w_ffn_gate"][0]), chunks(f["w_ffn_up"][0])], 1).reshape(-1, P, CH)
    w_ffn = np.concatenate([gu, chunks(f["w_ffn_down"][0])])

    def wide(w, n):
        t = w[:, 512 * n:512 * n + 512].reshape(-1, 2, P, 512)
        return t.transpose(0, 2, 1, 3).reshape(-1, P, CH)

    def down(w, n):
        return w[512 * n:512 * n + 512].reshape(4, P, CH)

    moe = []
    for e in range(NE):
        g, u, d = f["w_exp_gate"][0, e], f["w_exp_up"][0, e], f["w_exp_down"][0, e]
        moe += [wide(g, 0), wide(u, 0), wide(g, 1), wide(u, 1), down(d, 0), wide(g, 2), wide(u, 2), down(d, 1), down(d, 2)]
    moe.append(moe[0][:4])
    moe += [moe[1][:4], moe[2][:1]]
    w_moe = np.concatenate(moe)

    tokens = np.concatenate([f["meta_tokens"], f["x_prompt"][0], f["x_sample"].reshape(TS, D)])
    x_in = cols(tokens).transpose(0, 2, 1)

    p = np.arange(P)[:, None]

    def mask(s, w):
        i = np.arange(w)[None, :]
        return np.where((i >= s) & (i <= s + WIN), 0.0, -1e30)

    m_a = np.where(np.arange(128)[None, :] <= p, 0.0, -1e30)
    consts = np.concatenate([
        np.eye(P), np.ones((P, P)), np.tile(m_a, (1, 2)), mask(p, 256), mask(p % 16, 144), mask(p % 8, 136),
        (p < np.arange(P)[None, :]) * 1.0, np.broadcast_to(np.arange(SLOTS), (P, SLOTS)),
        np.broadcast_to(np.tile(NE - np.arange(NE), 3), (P, 24)),
        (p + 128 * np.repeat(np.arange(3), NE)[None, :] < T) * 1.0], axis=1).astype(np.float32)

    def sinks(s):
        s = s.reshape(2, 8)
        a = s.reshape(2, 4, 2).transpose(1, 0, 2).reshape(1, 16)
        b = s.T.reshape(1, 16)
        c = np.repeat(s, 16, axis=1).T
        d = np.repeat(s.reshape(-1), 8)[:, None]
        return np.concatenate([np.broadcast_to(a, (P, 16)), np.broadcast_to(b, (P, 16)), c, d, d], axis=1)

    par = np.stack([np.concatenate([
        cols(f["ln_mix"][l]), cols(f["ln_ffn"][l]), cols(f["w_conv"][l]).reshape(P, -1), cols(f["b_conv"][l]),
        cols(f["b_rg_a"][l]), cols(f["b_rg_i"][l]), cols(f["rg_lambda"][l]), sinks(f["attn_sinks"][l])], axis=1)
        for l in range(2)], axis=1)
    misc = np.concatenate([cols(f["ln_final"]), f["w_router"][0].reshape(KD, P, NE).transpose(1, 0, 2).reshape(P, -1),
                           np.broadcast_to(np.tile(f["b_router"][0], 3), (P, 24))], axis=1)
    state = np.stack([np.concatenate([
        cols(f["state_conv"][l]).transpose(0, 3, 1, 2).reshape(P, -1),
        cols(f["state_rglru"][l]).transpose(0, 2, 1).reshape(P, -1)], axis=1) for l in range(2)])
    kc = f["cache_k"].reshape(2, SB, WIN, P).transpose(0, 3, 1, 2)
    vc = f["cache_v"].reshape(2, SB, WIN, P).transpose(0, 2, 1, 3)

    ins = {"w_mix": w_mix, "w_ffn": w_ffn, "w_moe": w_moe, "x_in": x_in, "consts_in": consts, "par_in": par,
           "misc_in": misc, "state_in": state, "kc_in": kc, "vc_in": vc}
    outs = {"o_y": (P, KD, T), "o_kp": (2, P, WIN), "o_vp": (2, P, WIN), "o_ks": (2, P, SB, WIN),
            "o_vs": (2, WIN, SB, P), "o_state": (2, P, STATE_OUT)}
    nc = bacc.Bacc("TRN2", target_bir_lowering=False, num_devices=1)
    arrays = {k: np.ascontiguousarray(a) for k, a in ins.items()}
    args = [nc.dram_tensor(k, a.shape, F32, kind="ExternalInput").ap() for k, a in arrays.items()]
    args += [nc.dram_tensor(k, s, F32, kind="ExternalOutput").ap() for k, s in outs.items()]
    build_step(nc, *args)
    got = run_bass_kernel_spmd(nc, [arrays], core_ids=[0]).results[0]

    y = got["o_y"].transpose(2, 1, 0).reshape(T, D)
    st = got["o_state"]

    def rows(a, k):
        return a.reshape(2, P, KR, k).transpose(0, 3, 2, 1).reshape(2, k, REC)

    def kv(a):
        return a.transpose(0, 2, 1).reshape(2, 1, WIN, 2, HD)

    return (np.ascontiguousarray(y[META:TP])[None], np.ascontiguousarray(y[TP:]).reshape(SB, SS, D),
            kv(got["o_kp"]), kv(got["o_vp"]), rows(st[:, :, 0:30], 3)[:, None], rows(st[:, :, 270:280], 1),
            np.ascontiguousarray(got["o_ks"].transpose(0, 2, 3, 1)).reshape(2, SB, WIN, 2, HD),
            np.ascontiguousarray(got["o_vs"].transpose(0, 2, 1, 3)).reshape(2, SB, WIN, 2, HD),
            rows(st[:, :, 30:270], 24).reshape(2, SB, 3, REC), rows(st[:, :, 280:360], 8))
```
